# Optimizing a Trainium2 kernel written in Bass

```python
import jax, jax.numpy as jnp
from jax import lax
import numpy as np
import math
import jax
import jax.numpy as jnp

D_MODEL = 1024
BATCH = 1
SEQ = 256
DEPTH = 2

POOL_GROUPS = 4
POOL_GROUP_DIM = 128
POOL_WIDTH = POOL_GROUPS * POOL_GROUP_DIM
POOL_WINDOWS = (2, 4, 8, 16)
LRU_HEADS = 10
LRU_HEAD_DIM = 128
LRU_WIDTH = LRU_HEADS * LRU_HEAD_DIM
CONV_WIDTH = 4
LRU_C = 8.0
D_FF = 2816
EPS = 1e-6
IN_WIDTH = POOL_WIDTH + 2 * LRU_WIDTH + 2 * D_MODEL


def rmsnorm(x, g):
    xf = x.astype(jnp.float32)
    var = jnp.mean(xf * xf, axis=-1, keepdims=True)
    return (xf * lax.rsqrt(var + EPS) * g.astype(jnp.float32)).astype(x.dtype)

def swiglu_ffn(h, w_up, w_down):
    u = h @ w_up
    a, b = jnp.split(u, 2, axis=-1)
    return (jax.nn.silu(a) * b) @ w_down

def causal_pool_minus_self(u, window):
    b, s, c = u.shape
    uf = u.astype(jnp.float32)
    cs = jnp.cumsum(uf, axis=1)
    cs_pad = jnp.concatenate([jnp.zeros((b, 1, c), jnp.float32), cs], axis=1)
    prev = jnp.concatenate([jnp.zeros((b, window - 1, c), jnp.float32), cs_pad[:, : s - window + 1]], axis=1)
    count = jnp.minimum(jnp.arange(1, s + 1, dtype=jnp.float32), float(window))[None, :, None]
    return ((cs - prev) / count - uf).astype(u.dtype)

def pool_mixer(u, w_grp, b_grp, scale):
    b, s, _ = u.shape
    ug = u.reshape(b, s, POOL_GROUPS, POOL_GROUP_DIM)
    pooled = jnp.stack([causal_pool_minus_self(ug[:, :, g], POOL_WINDOWS[g]) for g in range(POOL_GROUPS)], axis=2)
    mixed = jnp.einsum('bsgc,gcd->bsgd', pooled, w_grp) + b_grp
    return mixed.reshape(b, s, POOL_WIDTH) * scale

def causal_depthwise_conv(u, w, bias):
    s = u.shape[1]
    up = jnp.pad(u, ((0, 0), (CONV_WIDTH - 1, 0), (0, 0)))
    y = sum(up[:, k:k + s] * w[k] for k in range(CONV_WIDTH))
    return y + bias

def _lru_combine(left, right):
    a_l, b_l = left
    a_r, b_r = right
    return a_l * a_r, a_r * b_l + b_r

def rg_lru(u, w_a, b_a, w_x, b_x, lam):
    b, s, _ = u.shape
    uh = u.reshape(b, s, LRU_HEADS, LRU_HEAD_DIM)
    r = jax.nn.sigmoid(jnp.einsum('bshd,hde->bshe', uh, w_a) + b_a).reshape(b, s, LRU_WIDTH)
    i = jax.nn.sigmoid(jnp.einsum('bshd,hde->bshe', uh, w_x) + b_x).reshape(b, s, LRU_WIDTH)
    log_a = -LRU_C * r.astype(jnp.float32) * jax.nn.softplus(-lam.astype(jnp.float32))
    a = jnp.exp(log_a)
    mult = jnp.sqrt(-jnp.expm1(2.0 * log_a))
    bx = mult * (i * u).astype(jnp.float32)
    _, h = lax.associative_scan(_lru_combine, (a, bx), axis=1)
    return h.astype(u.dtype)

def hybrid_mixer(h, w_in, pool_w, pool_b, pool_scale, w_pool_up, conv_w, conv_b,
                 lru_w_a, lru_b_a, lru_w_x, lru_b_x, lru_lambda, w_lru_up, w_out):
    proj = h @ w_in
    s1 = POOL_WIDTH
    s2 = s1 + LRU_WIDTH
    s3 = s2 + LRU_WIDTH
    u_pool, u_lru, u_gelu, g_logits = proj[..., :s1], proj[..., s1:s2], proj[..., s2:s3], proj[..., s3:]
    y_pool = pool_mixer(u_pool, pool_w, pool_b, pool_scale) @ w_pool_up
    v = causal_depthwise_conv(u_lru, conv_w, conv_b)
    y_lru = (rg_lru(v, lru_w_a, lru_b_a, lru_w_x, lru_b_x, lru_lambda) * jax.nn.gelu(u_gelu)) @ w_lru_up
    g = jax.nn.sigmoid(g_logits)
    g_pool, g_lru = g[..., :D_MODEL], g[..., D_MODEL:]
    return (g_pool * y_pool + g_lru * y_lru) @ w_out

def first_inputs(seed: int = 0) -> dict:
    key = jax.random.key(seed)
    ks = jax.random.split(key, 26)
    f32 = jnp.float32

    def nrm(k, shape, fan_in):
        return jax.random.normal(k, shape, f32) * (fan_in ** -0.5)

    def gain(k, shape):
        return 1.0 + 0.02 * jax.random.normal(k, shape, f32)

    def small(k, shape):
        return 0.01 * jax.random.normal(k, shape, f32)

    L = DEPTH
    a_c = jax.random.uniform(ks[17], (L, LRU_WIDTH), f32, 0.9, 0.999)
    sig = a_c ** (1.0 / LRU_C)
    lam = jnp.log(sig) - jnp.log1p(-sig)
    return {
        "x": jax.random.normal(ks[0], (BATCH, SEQ, D_MODEL), f32),
        "norm_ffn1": gain(ks[1], (L, D_MODEL)),
        "ffn1_w_up": nrm(ks[2], (L, D_MODEL, 2 * D_FF), D_MODEL),
        "ffn1_w_down": nrm(ks[3], (L, D_FF, D_MODEL), D_FF),
        "norm_mix": gain(ks[4], (L, D_MODEL)),
        "w_in": nrm(ks[5], (L, D_MODEL, IN_WIDTH), D_MODEL),
        "pool_w": nrm(ks[6], (L, POOL_GROUPS, POOL_GROUP_DIM, POOL_GROUP_DIM), POOL_GROUP_DIM),
        "pool_b": small(ks[7], (L, POOL_GROUPS, POOL_GROUP_DIM)),
        "pool_scale": 1.0 + 0.1 * jax.random.normal(ks[8], (L, POOL_WIDTH), f32),
        "w_pool_up": nrm(ks[9], (L, POOL_WIDTH, D_MODEL), POOL_WIDTH),
        "conv_w": nrm(ks[10], (L, CONV_WIDTH, LRU_WIDTH), CONV_WIDTH),
        "conv_b": small(ks[11], (L, LRU_WIDTH)),
        "lru_w_a": nrm(ks[12], (L, LRU_HEADS, LRU_HEAD_DIM, LRU_HEAD_DIM), LRU_HEAD_DIM),
        "lru_b_a": small(ks[13], (L, LRU_HEADS, LRU_HEAD_DIM)),
        "lru_w_x": nrm(ks[14], (L, LRU_HEADS, LRU_HEAD_DIM, LRU_HEAD_DIM), LRU_HEAD_DIM),
        "lru_b_x": small(ks[15], (L, LRU_HEADS, LRU_HEAD_DIM)),
        "lru_lambda": lam,
        "w_lru_up": nrm(ks[16], (L, LRU_WIDTH, D_MODEL), LRU_WIDTH),
        "w_out": nrm(ks[18], (L, D_MODEL, D_MODEL), D_MODEL),
        "norm_ffn2": gain(ks[19], (L, D_MODEL)),
        "ffn2_w_up": nrm(ks[20], (L, D_MODEL, 2 * D_FF), D_MODEL),
        "ffn2_w_down": nrm(ks[21], (L, D_FF, D_MODEL), D_FF),
        "final_norm": gain(ks[22], (D_MODEL,)),
    }

def first_block(x, norm_ffn1, ffn1_w_up, ffn1_w_down, norm_mix, w_in, pool_w, pool_b, pool_scale,
              w_pool_up, conv_w, conv_b, lru_w_a, lru_b_a, lru_w_x, lru_b_x, lru_lambda, w_lru_up,
              w_out, norm_ffn2, ffn2_w_up, ffn2_w_down, final_norm):
    for l in range(DEPTH):
        x = x + 0.5 * swiglu_ffn(rmsnorm(x, norm_ffn1[l]), ffn1_w_up[l], ffn1_w_down[l])
        x = x + hybrid_mixer(rmsnorm(x, norm_mix[l]), w_in[l], pool_w[l], pool_b[l], pool_scale[l],
                             w_pool_up[l], conv_w[l], conv_b[l], lru_w_a[l], lru_b_a[l],
                             lru_w_x[l], lru_b_x[l], lru_lambda[l], w_lru_up[l], w_out[l])
        x = x + 0.5 * swiglu_ffn(rmsnorm(x, norm_ffn2[l]), ffn2_w_up[l], ffn2_w_down[l])
    return rmsnorm(x, final_norm)


GRID_W = 64
CTX_LEN = 256
N_MIXERS = 2
RMS_EPS = 1e-6

RW_HEAD = 64
RW_WIDTH = D_MODEL
RW_HEADS = RW_WIDTH // RW_HEAD
W_LORA = 64
A_LORA = 64
RW_IN_COLS = 4 * RW_WIDTH + 2 * (W_LORA + A_LORA)
RW_MIX_COLS = 3 * RW_WIDTH + 2 * (W_LORA + A_LORA)
GN_EPS = 64e-5

DA_HEADS = 8
DA_HEAD = 64
DA_VHEAD = 2 * DA_HEAD
DA_QW = DA_HEADS * 2 * DA_HEAD
DA_VW = DA_HEADS * DA_VHEAD
DA_GW = DA_VW
DA_IN_COLS = 2 * DA_QW + DA_VW + DA_GW
SUBLN_EPS = 1e-5
ROPE_THETA = 10000.0
ROPE_FREQS = DA_HEAD // 4
Q_BLOCK = 128

N_A = (DEPTH + 1) // 2
N_B = DEPTH // 2


def rms_norm(x, g, eps=RMS_EPS):
    xf = x.astype(jnp.float32)
    y = xf * lax.rsqrt(jnp.mean(xf * xf, axis=-1, keepdims=True) + eps)
    return (y * g.astype(jnp.float32)).astype(x.dtype)

def centred_token_shift(u, mu):
    prev = jnp.pad(u[:, :-1], ((0, 0), (1, 0), (0, 0)))
    nxt = jnp.pad(u[:, 1:], ((0, 0), (0, 1), (0, 0)))
    return u + mu * (0.5 * (prev + nxt) - u)

def rwkv7_streams(h, w_in, mu, w0, w2, a0, a2, k_k, k_a):
    B, T, _ = h.shape
    C = RW_WIDTH
    heads = lambda t: t.reshape(t.shape[:-1] + (RW_HEADS, RW_HEAD))
    proj = (h @ w_in).astype(jnp.float32)
    g = proj[..., 3 * C:4 * C]
    mixed = centred_token_shift(
        jnp.concatenate([proj[..., :3 * C], proj[..., 4 * C:]], axis=-1), mu.astype(jnp.float32))
    r, k, v = mixed[..., :C], mixed[..., C:2 * C], mixed[..., 2 * C:3 * C]
    lw = mixed[..., 3 * C:3 * C + 2 * W_LORA].reshape(B, T, 2, W_LORA)
    la = mixed[..., 3 * C + 2 * W_LORA:].reshape(B, T, 2, A_LORA)
    w_raw = w0 + jnp.einsum("btdr,drc->btdc", jnp.tanh(lw), w2)
    decay = jnp.exp(-jnp.exp(-jax.nn.softplus(-w_raw) - 0.5))
    a = jax.nn.sigmoid(a0 + jnp.einsum("btdr,drc->btdc", la, a2))
    kk = heads(k * k_k)
    kk = kk * lax.rsqrt(jnp.sum(kk * kk, axis=-1, keepdims=True) + 1e-12)
    kd = k[:, :, None, :] * (1.0 + (a - 1.0) * k_a)
    return heads(r), heads(v), kk, heads(decay), heads(a), heads(kd), g

def wkv_scan(r, w, k, v, kk, a, s0, reverse):
    xs = tuple(jnp.moveaxis(t, 1, 0) for t in (r, w, k, v, kk, a))

    def step(S, inp):
        r_t, w_t, k_t, v_t, kk_t, a_t = inp
        sa = jnp.einsum("bhvk,bhk->bhv", S, kk_t)
        S = (S * w_t[:, :, None, :]
             - sa[..., None] * (kk_t * a_t)[:, :, None, :]
             + v_t[..., None] * k_t[:, :, None, :])
        return S, jnp.einsum("bhvk,bhk->bhv", S, r_t)

    s_fin, o = lax.scan(step, s0, xs, reverse=reverse)
    return jnp.moveaxis(o, 0, 1), s_fin

def scan_direction(streams, d, s0, reverse):
    r, v, kk, decay, a, kd, _ = streams
    return wkv_scan(r, decay[:, :, d], kd[:, :, d], v, kk, a[:, :, d], s0, reverse)

def rwkv7_readout(o, streams, r_k, gn_g, gn_b, w_out, out_dtype):
    r, v, _, _, _, kd, g = streams
    B, T = o.shape[:2]
    mean = jnp.mean(o, axis=-1, keepdims=True)
    var = jnp.mean(jnp.square(o - mean), axis=-1, keepdims=True)
    y = ((o - mean) * lax.rsqrt(var + GN_EPS)).reshape(B, T, RW_WIDTH) * gn_g + gn_b
    bonus = jnp.sum(jnp.sum(r[:, :, None] * kd * r_k, axis=-1, keepdims=True) * v[:, :, None], axis=2)
    y = (y + bonus.reshape(B, T, RW_WIDTH)) * jax.nn.silu(g)
    return y.astype(out_dtype) @ w_out

def rwkv7_mixer(h, hc, w_in, mu, w0, w2, a0, a2, k_k, k_a, r_k, gn_g, gn_b, w_out, ctx_out):
    lat = rwkv7_streams(h, w_in, mu, w0, w2, a0, a2, k_k, k_a)
    con = rwkv7_streams(hc, w_in, mu, w0, w2, a0, a2, k_k, k_a)
    s0 = jnp.zeros((h.shape[0], RW_HEADS, RW_HEAD, RW_HEAD), jnp.float32)
    oc_f, sc_f = scan_direction(con, 0, s0, False)
    oc_b, sc_b = scan_direction(con, 1, s0, True)
    ol_f, _ = scan_direction(lat, 0, sc_f, False)
    ol_b, _ = scan_direction(lat, 1, sc_b, True)
    y = rwkv7_readout(ol_f + ol_b, lat, r_k, gn_g, gn_b, w_out, h.dtype)
    yc = rwkv7_readout(oc_f + oc_b, con, r_k, gn_g, gn_b, w_out, hc.dtype) if ctx_out else None
    return y, yc

def axial_rope_tables(rows):
    row_ids = jnp.repeat(jnp.arange(rows), GRID_W).astype(jnp.float32)
    col_ids = jnp.tile(jnp.arange(GRID_W), rows).astype(jnp.float32)
    inv_freq = ROPE_THETA ** (-jnp.arange(ROPE_FREQS, dtype=jnp.float32) / ROPE_FREQS)
    ang = jnp.stack([row_ids[:, None] * inv_freq, col_ids[:, None] * inv_freq], axis=1)
    return jnp.cos(ang), jnp.sin(ang)

def apply_axial_rope(x, cos, sin):
    xr = x.reshape(x.shape[:-1] + (2, 2, ROPE_FREQS))
    x1, x2 = xr[..., 0, :], xr[..., 1, :]
    c = cos[None, :, None, None].astype(x.dtype)
    s = sin[None, :, None, None].astype(x.dtype)
    out = jnp.stack([x1 * c - x2 * s, x2 * c + x1 * s], axis=-2)
    return out.reshape(x.shape)

def diff_attention_blocks(q, k_all, v_all, lam):
    B, T = q.shape[:2]
    nb = T // Q_BLOCK
    qb = jnp.moveaxis(q.reshape((B, nb, Q_BLOCK) + q.shape[2:]), 1, 0)
    scale = DA_HEAD ** -0.5

    def block(q_blk):
        s = jnp.einsum("bqhcd,bkhcd->bchqk", q_blk, k_all).astype(jnp.float32) * scale
        p = jax.nn.softmax(s, axis=-1)
        attn = p[:, 0] - lam * p[:, 1]
        return jnp.einsum("bhqk,bkhe->bqhe", attn.astype(v_all.dtype), v_all)

    o = lax.map(block, qb)
    return jnp.moveaxis(o, 0, 1).reshape(B, T, DA_HEADS, DA_VHEAD)

def diff_finish(o, g, subln, lam_init, w_out):
    B, T = o.shape[:2]
    y = rms_norm(o, subln, SUBLN_EPS) * (1.0 - lam_init)
    return (y.reshape(B, T, DA_VW) * jax.nn.silu(g)) @ w_out

def diff_mixer(h, hc, layer_idx, w_in, qn, kn, lam_vecs, subln, w_out, cos, sin, ctx_out):
    B, T, _ = h.shape
    Lc = hc.shape[1]
    lam_init = 0.8 - 0.6 * math.exp(-0.3 * layer_idx)
    lv = lam_vecs.astype(jnp.float32)
    lam = jnp.exp(jnp.sum(lv[0] * lv[1])) - jnp.exp(jnp.sum(lv[2] * lv[3])) + lam_init
    proj = h @ w_in
    q = apply_axial_rope(rms_norm(proj[..., :DA_QW].reshape(B, T, DA_HEADS, 2, DA_HEAD), qn), cos, sin)
    k = apply_axial_rope(rms_norm(proj[..., DA_QW:2 * DA_QW].reshape(B, T, DA_HEADS, 2, DA_HEAD), kn), cos, sin)
    v = proj[..., 2 * DA_QW:2 * DA_QW + DA_VW].reshape(B, T, DA_HEADS, DA_VHEAD)
    g = proj[..., 2 * DA_QW + DA_VW:]
    if ctx_out:
        pc = hc @ w_in
        kvc = pc[..., DA_QW:2 * DA_QW + DA_VW]
    else:
        kvc = hc @ w_in[:, DA_QW:2 * DA_QW + DA_VW]
    kc = rms_norm(kvc[..., :DA_QW].reshape(B, Lc, DA_HEADS, 2, DA_HEAD), kn)
    vc = kvc[..., DA_QW:].reshape(B, Lc, DA_HEADS, DA_VHEAD)
    k_all = jnp.concatenate([kc, k], axis=1)
    v_all = jnp.concatenate([vc, v], axis=1)
    y = diff_finish(diff_attention_blocks(q, k_all, v_all, lam), g, subln, lam_init, w_out)
    yc = None
    if ctx_out:
        qc = rms_norm(pc[..., :DA_QW].reshape(B, Lc, DA_HEADS, 2, DA_HEAD), qn)
        yc = diff_finish(diff_attention_blocks(qc, kc, vc, lam), pc[..., 2 * DA_QW + DA_VW:],
                         subln, lam_init, w_out)
    return y, yc

def second_inputs(seed: int = 0) -> dict:
    key = jax.random.key(seed)
    ks = jax.random.split(key, 26)
    f32 = jnp.float32
    nrm = lambda k, shape, s: jax.random.normal(k, shape, f32) * s
    D = D_MODEL
    return {
        "x": nrm(ks[0], (BATCH, SEQ, D), 1.0),
        "c": nrm(ks[1], (BATCH, D), 1.0),
        "ctx": nrm(ks[2], (BATCH, CTX_LEN, D), 1.0),
        "c_ctx": nrm(ks[3], (D,), 1.0),
        "ada_w": nrm(ks[4], (DEPTH, D, 3 * D), 0.5 * D ** -0.5),
        "ada_b": nrm(ks[5], (DEPTH, 3 * D), 0.02),
        "norm_g": 1.0 + nrm(ks[6], (DEPTH, D), 0.02),
        "rw_in": nrm(ks[7], (N_A, D, RW_IN_COLS), D ** -0.5),
        "rw_mu": jax.random.uniform(ks[8], (N_A, RW_MIX_COLS), f32),
        "rw_w0": jax.random.uniform(ks[9], (N_A, 2, RW_WIDTH), f32, minval=-6.0, maxval=-1.0),
        "rw_w2": nrm(ks[10], (N_A, 2, W_LORA, RW_WIDTH), 0.1 * W_LORA ** -0.5),
        "rw_a0": nrm(ks[11], (N_A, 2, RW_WIDTH), 0.1),
        "rw_a2": nrm(ks[12], (N_A, 2, A_LORA, RW_WIDTH), 0.1 * A_LORA ** -0.5),
        "rw_kk": 0.85 + nrm(ks[13], (N_A, RW_WIDTH), 0.05),
        "rw_ka": 1.0 + nrm(ks[14], (N_A, RW_WIDTH), 0.05),
        "rw_rk": nrm(ks[15], (N_A, RW_HEADS, RW_HEAD), 0.1),
        "rw_gn_g": 1.0 + nrm(ks[16], (N_A, RW_WIDTH), 0.02),
        "rw_gn_b": nrm(ks[17], (N_A, RW_WIDTH), 0.02),
        "rw_out": nrm(ks[18], (N_A, RW_WIDTH, D), RW_WIDTH ** -0.5),
        "da_in": nrm(ks[19], (N_B, D, DA_IN_COLS), D ** -0.5),
        "da_qn": 1.0 + nrm(ks[20], (N_B, DA_HEAD), 0.02),
        "da_kn": 1.0 + nrm(ks[21], (N_B, DA_HEAD), 0.02),
        "da_lam": nrm(ks[22], (N_B, 4, DA_HEAD), 0.1),
        "da_subln": 1.0 + nrm(ks[23], (N_B, DA_VHEAD), 0.02),
        "da_out": nrm(ks[24], (N_B, DA_VW, D), DA_VW ** -0.5),
    }

def second_block(x, c, ctx, c_ctx, ada_w, ada_b, norm_g, rw_in, rw_mu, rw_w0, rw_w2, rw_a0, rw_a2,
              rw_kk, rw_ka, rw_rk, rw_gn_g, rw_gn_b, rw_out, da_in, da_qn, da_kn, da_lam,
              da_subln, da_out):
    n_lat = x.shape[1]
    rows = n_lat // GRID_W
    cos, sin = axial_rope_tables(rows)
    xc = ctx
    for i in range(DEPTH):
        last = i == DEPTH - 1
        j = i // N_MIXERS
        mod = jax.nn.silu(c) @ ada_w[i] + ada_b[i]
        shift, scale, gate = jnp.split(mod[:, None, :], 3, axis=-1)
        modc = jax.nn.silu(c_ctx) @ ada_w[i] + ada_b[i]
        shift_c, scale_c, gate_c = jnp.split(modc, 3)
        h = rms_norm(x, norm_g[i]) * (1.0 + scale) + shift
        hc = rms_norm(xc, norm_g[i]) * (1.0 + scale_c) + shift_c
        if i % N_MIXERS == 0:
            y, yc = rwkv7_mixer(h, hc, rw_in[j], rw_mu[j], rw_w0[j], rw_w2[j], rw_a0[j], rw_a2[j],
                                rw_kk[j], rw_ka[j], rw_rk[j], rw_gn_g[j], rw_gn_b[j], rw_out[j],
                                not last)
        else:
            y, yc = diff_mixer(h, hc, i, da_in[j], da_qn[j], da_kn[j], da_lam[j], da_subln[j],
                               da_out[j], cos, sin, not last)
        x = x + gate * y
        if not last:
            xc = xc + gate_c * yc
    return x


def setup_inputs(seed=0):
    out = dict(first_inputs(seed))
    for name, value in second_inputs(seed + 1).items():
        if name != "x":
            out[name + "_2"] = value
    return out


def reference(
    x, norm_ffn1, ffn1_w_up, ffn1_w_down, norm_mix, w_in, pool_w, pool_b, pool_scale, w_pool_up,
    conv_w, conv_b, lru_w_a, lru_b_a, lru_w_x, lru_b_x, lru_lambda, w_lru_up, w_out, norm_ffn2,
    ffn2_w_up, ffn2_w_down, final_norm, c_2, ctx_2, c_ctx_2, ada_w_2, ada_b_2, norm_g_2,
    rw_in_2, rw_mu_2, rw_w0_2, rw_w2_2, rw_a0_2, rw_a2_2, rw_kk_2, rw_ka_2, rw_rk_2, rw_gn_g_2,
    rw_gn_b_2, rw_out_2, da_in_2, da_qn_2, da_kn_2, da_lam_2, da_subln_2, da_out_2,
):
    x = first_block(
        x, norm_ffn1, ffn1_w_up, ffn1_w_down, norm_mix, w_in, pool_w, pool_b, pool_scale,
        w_pool_up, conv_w, conv_b, lru_w_a, lru_b_a, lru_w_x, lru_b_x, lru_lambda, w_lru_up,
        w_out, norm_ffn2, ffn2_w_up, ffn2_w_down, final_norm,
    )
    return second_block(
        x, c_2, ctx_2, c_ctx_2, ada_w_2, ada_b_2, norm_g_2, rw_in_2, rw_mu_2, rw_w0_2, rw_w2_2,
        rw_a0_2, rw_a2_2, rw_kk_2, rw_ka_2, rw_rk_2, rw_gn_g_2, rw_gn_b_2, rw_out_2, da_in_2,
        da_qn_2, da_kn_2, da_lam_2, da_subln_2, da_out_2,
    )


_drawn_inputs = setup_inputs


def setup_inputs(seed=0):
    import zlib

    import numpy as np

    out = dict(_drawn_inputs(seed))
    spreads = {}
    factors = {'norm_ffn1': 4.375,
     'norm_mix': 3.768,
     'pool_b': 6.376,
     'conv_b': 3.109,
     'lru_b_a': 8.0,
     'lru_b_x': 8.0,
     'norm_ffn2': 5.512,
     'final_norm': 2.673,
     'norm_g_2': 6.323,
     'rw_w2_2': 64.0,
     'rw_a0_2': 6.805,
     'rw_a2_2': 7.511,
     'rw_ka_2': 2.861,
     'rw_gn_g_2': 64.0,
     'rw_gn_b_2': 64.0,
     'da_qn_2': 64.0,
     'da_kn_2': 64.0,
     'da_lam_2': 5.321,
     'da_subln_2': 64.0,
     'rw_kk_2': 8.0}
    for name, (base, spread) in spreads.items():
        noise = np.random.default_rng([zlib.crc32(name.encode()), seed]).standard_normal(out[name].shape)
        drawn = base * np.exp(spread * noise) if base else spread * noise
        out[name] = jnp.asarray(drawn.astype(out[name].dtype))
    for name, factor in factors.items():
        out[name] = (out[name] * factor).astype(out[name].dtype)
    return out
```

```python
import math

import numpy as np

import concourse.bass as bass
from concourse import mybir

F32 = mybir.dt.float32
ALU = mybir.AluOpType
ACT = mybir.ActivationFunctionType
AX_X = mybir.AxisListType.X

P = 128
D = 1024
DC = D // P
T = 256
EPS = 1e-6

LAYERS = 2
FF = 2816
FC = FF // P
PG = 4
WINDOWS = (2, 4, 8, 16)
PAD = 16
LH = 10
CONV = 4
LRU_C = 8.0

SLOT_TILES = 16
RING = 5
BANKS = 8


def slots_of(tiles):
    return -(-tiles // (SLOT_TILES * RING)) * RING


FIRST_TILES = 2 * 3 * FC * DC + (PG + 2 * LH + 2 * DC) * DC + 2 * LH + PG + PG * DC + LH * DC + DC * DC
FIRST_SLOTS = slots_of(FIRST_TILES)


def columns(*sizes):
    at, n = {}, 0
    for name, size in sizes:
        at[name] = n
        n += size
    return at, n


P1, NP1 = columns(("norm_ffn1", DC), ("norm_mix", DC), ("norm_ffn2", DC), ("pool_b", PG), ("pool_scale", PG),
                  ("conv_w", CONV * LH), ("conv_b", LH), ("b_a", LH), ("b_x", LH))


HEAD = 64
PAIRS = D // (2 * HEAD)
LORA = 64
T2 = 2 * T
GN_EPS = 64e-5
DECAY = math.exp(-0.5)
CHUNK = 64
STEPS = T2 // CHUNK
LEVELS = 6
GROUPS = STEPS // 2
U_BANKS = ((0, 0), (1, 0))

DA_HEADS = 8
GRID_W = 64
ROPE_FREQS = HEAD // 4
ROPE_THETA = 10000.0
SUBLN_EPS = 1e-5
LAM_INIT = 0.8 - 0.6 * math.exp(-0.3 * 1)
SCALE = HEAD ** -0.5

P2, NP2 = columns(("norm_g", 2 * DC), ("ada_b", 2 * 3 * DC), ("mu", 3 * DC + 2), ("w0", 2 * DC), ("a0", 2 * DC),
                  ("kk", DC), ("ka", DC), ("rk", DC), ("gn_g", DC), ("gn_b", DC), ("qn", 1), ("kn", 1), ("subln", 1))

MOD_CHUNKS = 4
MOD_TILES = 3 * DC // MOD_CHUNKS

SECOND_A_TILES = (4 * DC + 2) * DC
SECOND_B_TILES = DC * DC + 4 * DC * DC + DC * DC
SECOND_A_SLOTS, SECOND_B_SLOTS = slots_of(SECOND_A_TILES), slots_of(SECOND_B_TILES)
RING_AT_REST = RING + LAYERS * FIRST_SLOTS + SECOND_A_SLOTS


def constants():
    t = np.arange(T)
    inv = np.stack([1.0 / np.minimum(t + 1, w) for w in WINDOWS])
    i = np.arange(CHUNK)
    table = {
        "inv_count": np.broadcast_to(inv.reshape(1, -1), (P, PG * T)),
        "identity": np.eye(P),
        "same_head": np.kron(np.eye(2), np.ones((HEAD, HEAD))),
        "earlier": np.tile(i[:, None] < i[None, :], (2, 1)),
        "writes_before": np.tile(np.concatenate([i[:, None] < i[None, :], i[:, None] <= i[None, :]], 1), (2, 1)),
    }
    for level in range(LEVELS):
        b = 1 << level
        below = (i[:, None] // (2 * b) == i[None, :] // (2 * b)) & (i[:, None] // b % 2 == 1) & (i[None, :] // b % 2 == 0)
        if level == 0:
            table["minus_below0"] = np.tile(-1.0 * below, (2, 1))
            table["minus_above0"] = np.tile(-1.0 * below.T, (2, 1))
        else:
            table[f"below{level}"] = np.tile(below, (2, 1))
    f = np.arange(HEAD)
    freq = ROPE_THETA ** (-(f % ROPE_FREQS).astype(np.float32) / ROPE_FREQS)
    place = np.where((f // (2 * ROPE_FREQS) == 0)[:, None], (t // GRID_W)[None], (t % GRID_W)[None])
    angle = (place.astype(np.float32) * freq.astype(np.float32)[:, None]).astype(np.float32)
    turn = np.zeros((HEAD, HEAD))
    for m in range(HEAD):
        if f[m] // ROPE_FREQS % 2 == 0:
            turn[m + ROPE_FREQS, m] = -1.0
        else:
            turn[m - ROPE_FREQS, m] = 1.0
    table.update(rope_turn=np.kron(np.eye(2), turn), rope_cos=np.tile(np.cos(angle), (2, 1)),
                 rope_sin=np.tile(np.sin(angle), (2, 1)))
    return {k: np.asarray(v, np.float32) for k, v in table.items()}


CONST = constants()
C_AT, C_COLS = columns(*((k, v.shape[1]) for k, v in CONST.items()))


class Order:

    def __init__(self, after=None, turns=1, banks=range(BANKS)):
        self.after, self.turns, self.banks = after, turns, list(banks)
        self.place, self.taken_by = {}, {}
        self.names = []
        self.count = {"dve": 0, "act": 0}
        self.full0 = 0 if after is None else after.full0 + after.turns * len(after.names)
        self.taken0 = None if after is None else {
            e: after.taken0[e] + after.turns * after.count[e] for e in ("dve", "act")}

    def add(self, name, by):
        self.count[by] += 1
        self.taken_by[name] = by, self.count[by]
        self.place[name] = len(self.names)
        self.names.append(name)

    def close(self):
        if self.after is None:
            self.taken0 = dict(self.count)
        return self

    def bank(self, name):
        return self.banks[self.place[name] % len(self.banks)]

    def full(self, name, turn=0):
        return self.full0 + turn * len(self.names) + self.place[name] + 1

    def taken(self, name, turn=0):
        by, n = self.taken_by[name]
        return self.taken0[by] + turn * self.count[by] + n

    def one_round_before(self, name, turn=0):
        place = self.place[name] - len(self.banks)
        if place >= 0:
            name = self.names[place]
            return self.taken_by[name][0], self.taken(name, turn)
        if self.after is not None:
            return None
        bank = self.bank(name)
        name = [n for i, n in enumerate(self.names) if i % len(self.banks) == bank][-1]
        return self.taken_by[name][0], self.taken(name, turn - 1)


MOD_AFTER = (FC // 2, FC - 1)
MOD_BEFORE = ("pool_up", "w_out")


def first_order():
    o = Order(turns=LAYERS)

    def feed_forward(ffn):
        for j in range(FC):
            o.add((ffn, "a", j), "dve")
            if j == 0:
                o.add((ffn, "mean_square"), "act")
            o.add((ffn, "b", j), "dve")
            if j in MOD_AFTER:
                o.add(("mod", MOD_AFTER.index(j) + (0 if ffn == "ffn1" else 4)), "dve")
        for m in range(DC):
            o.add((ffn, "down", m), "dve")

    feed_forward("ffn1")
    for h in range(LH):
        o.add(("u_lru", h), "dve")
        if h == 0:
            o.add(("mix", "mean_square"), "act")
    for g in range(PG):
        o.add(("u_pool", g), "dve")
    for h in range(LH):
        o.add(("u_gelu", h), "dve")
    for h in range(LH):
        o.add(("gate_a", h), "act")
        o.add(("gate_x", h), "act")
    for m in range(2 * DC):
        o.add(("g_logit", m), "dve")
        if m < PG:
            o.add(("pool_mix", m), "dve")
    for name in ("pool_up", "lru_up", "w_out"):
        if name in MOD_BEFORE:
            o.add(("mod", 2 + MOD_BEFORE.index(name)), "dve")
        for m in range(DC):
            o.add((name, m), "dve")
    feed_forward("ffn2")
    return o.close()


FIRST = first_order()
FIRST_STEPS = 107


def second_a_order():
    o = Order(FIRST)
    o.add(("final", "mean_square"), "act")
    o.add(("rw", "mean_square"), "act")
    for m in (4 * DC, 4 * DC + 1, *range(3 * DC), *range(3 * DC, 4 * DC)):
        o.add(("rw_in", m), "act")
    return o.close()


SECOND_A = second_a_order()


def scan_side_tiles(q):
    pair, g = divmod(q, GROUPS)
    inside, ahead, behind = 0 <= pair < PAIRS, pair + 1 < PAIRS, pair >= 1
    names = [("bk_turned", q, "act"), ("v_turned", q, "act")] if inside else []
    names += [("kv", q, "act")] if inside else []
    if g == 0 and ahead:
        names += [("kk_norm", pair + 1, "act"), ("w", pair + 1, 0, "act"), ("a", pair + 1, 0, "act")]
    if g == 1 and ahead:
        names += [("w", pair + 1, 1, "act"), ("a", pair + 1, 1, "act")]
    if g == 1 and behind:
        names += [("o_mean", pair - 1, "dve")]
    if g == 2 and behind:
        names += [("o_var", pair - 1, "act")]
    if g == 3 and 0 <= pair and ahead:
        names += [("bonus", pair + 1, "dve")]
    if q == 0:
        names += [("bonus", 0, "dve")]
    return names


def scan_order():
    o = Order(SECOND_A, banks=(6, 7))
    for q in range(-GROUPS, (PAIRS + 1) * GROUPS):
        for *name, by in scan_side_tiles(q):
            o.add(tuple(name), by)
    return o.close()


SCAN = scan_order()

STEP_PLACES = (("start",), ("t1", 1), ("xy", 1), ("xy", 2), ("t1", 3), ("t1", 4))


def second_b_order():
    o = Order(SCAN)
    for m in range(DC):
        o.add(("rw_out", m), "dve")
    o.add(("da", "mean_square"), "act")
    for kind in ("k", "q"):
        for h in range(DA_HEADS + 2):
            if h < DA_HEADS:
                o.add((kind, h), "act")
            if 1 <= h <= DA_HEADS:
                o.add((kind + "_mean_square", h - 1), "act")
            if h >= 2:
                o.add((kind + "_turned", h - 2), "dve")
    for h in range(DA_HEADS + 1):
        if h < DA_HEADS:
            o.add(("v", h), "act")
        if h >= 1:
            o.add(("v_turned", h - 1), "act")
    for h in range(DA_HEADS):
        o.add(("g", h), "act")
    o.add(("lam",), "act")
    for i in range(-1, 2 * DA_HEADS + 1):
        if i + 1 < 2 * DA_HEADS:
            o.add(("scores", i + 1, 0), "act")
            o.add(("scores", i + 1, 1), "act")
        if i >= 1:
            o.add(("probs_turned", i - 1), "dve")
        if i >= 2 and i % 2 == 0:
            o.add(("o", i // 2 - 1), "dve")
    for h in range(DA_HEADS):
        o.add(("o_mean_square", h), "act")
    for m in range(DC):
        o.add(("da_out", m), "dve")
    return o.close()


SECOND_B = second_b_order()


class Semaphores:

    def __init__(self, nc):
        new = nc.alloc_semaphore
        self.slot_landed = [new(f"slot_landed_{r}") for r in range(RING)]
        self.bank_full = new("bank_full")
        self.slot_used = new("slot_used")
        self.loaded = new("loaded")
        self.stored = new("stored")
        self.tables_loaded = new("tables_loaded")
        self.tables_ready = new("tables_ready")
        self.dve_taken = new("dve_taken")
        self.act_taken = new("act_taken")
        self.dve_chain = new("dve_chain")
        self.x_scaled = new("x_scaled")
        self.x_squared = new("x_squared")
        self.gate_silu = new("gate_silu")
        self.hidden_written = new("hidden_written")
        self.conv_written = new("conv_written")
        self.gelu_done = new("gelu_done")
        self.lru_tanh_done = new("lru_tanh_done")
        self.lru_root_done = new("lru_root_done")
        self.lru_out_written = new("lru_out_written")
        self.g_done = new("g_done")
        self.pooled_written = new("pooled_written")
        self.y_written = new("y_written")
        self.log_done = new("log_done")
        self.c_silu = new("c_silu")
        self.mod_landed = [new(f"mod_landed_{b}") for b in range(2)]
        self.mod_product = new("mod_product")
        self.mod_summed = new("mod_summed")
        self.context_loaded = new("context_loaded")
        self.x_normed = new("x_normed")
        self.sq_ready = new("sq_ready")
        self.h_ready = new("h_ready")
        self.mixed = new("mixed")
        self.lora_in = new("lora_in")
        self.kk_scaled = new("kk_scaled")
        self.kk_squared = new("kk_squared")
        self.wa_ready = new("wa_ready")
        self.kk_inverse = new("kk_inverse")
        self.o_inverse = new("o_inverse")
        self.products_ready = new("products_ready")
        self.pool_chain = new("pool_chain")
        self.kk_normed = new("kk_normed")
        self.first_backward_ready = new("first_backward_ready")
        self.spread_ready = new("spread_ready")
        self.pair_ready = new("pair_ready")
        self.bonus_in = new("bonus_in")
        self.o_summed = new("o_summed")
        self.o_squared = new("o_squared")
        self.y_ready = new("y_ready")
        self.reversed_ready = new("reversed_ready")
        self.out_squared = new("out_squared")
        self.squared = new("squared")
        self.scaled = new("scaled")
        self.q_zeroed = new("q_zeroed")
        self.turned_in = new("turned_in")
        self.lam_in = new("lam_in")
        self.max_ready = new("max_ready")
        self.probs_ready = new("probs_ready")
        self.o_squared2 = new("o_squared2")
        self.attn_ready = new("attn_ready")
        self.gram_full = new("gram_full")
        self.stack_full = new("stack_full")
        self.gram_taken = new("gram_taken")
        self.t1_full = new("t1_full")
        self.t1_masked = new("t1_masked")
        self.xy_full = new("xy_full")
        self.xy_updated = new("xy_updated")
        self.z_full = new("z_full")
        self.z_taken = new("z_taken")
        self.u_full = new("u_full")
        self.u_taken = new("u_taken")
        self.os_full = new("os_full")
        self.o_taken = new("o_taken")
        self.s_updated = new("s_updated")


class Arena:

    def __init__(self, whole, at=0):
        self.whole, self.at = whole, at
        self.size = whole.shape[1]

    def take(self, *shape):
        n = math.prod(shape)
        assert self.at + n <= self.size, (self.at, n, self.size)
        part = self.whole[:, self.at:self.at + n]
        self.at += n
        if len(shape) == 2:
            return part.rearrange("p (a b) -> p a b", a=shape[0])
        if len(shape) == 3:
            return part.rearrange("p (a b c) -> p a b c", a=shape[0], b=shape[1])
        if len(shape) == 4:
            return part.rearrange("p (a b c d) -> p a b c d", a=shape[0], b=shape[1], c=shape[2])
        return part


class Chain:

    def __init__(self, eng, sem):
        self.eng, self.sem, self.base, self.n = eng, sem, 0, 0

    def start(self, base):
        self.base, self.n = base, 0

    def __call__(self, ins):
        self.n += 1
        ins.then_inc(self.sem, 1)
        self.eng.wait_ge(self.sem, self.base + self.n)


class PeStream:

    def __init__(self, nc, pe, ring, psum, s):
        self.nc, self.pe, self.ring, self.psum, self.s = nc, pe, ring, psum, s
        self.to_release = 0

    def start(self, order, turn=0):
        self.order, self.turn = order, turn

    def weights_from(self, ring_turns):
        self.ring_turns, self.k = ring_turns, 0

    def all_banks_empty(self, order):
        self.pe.wait_ge(self.s.dve_taken, order.taken0["dve"])
        self.pe.wait_ge(self.s.act_taken, order.taken0["act"])

    def bank(self, name, n=T):
        left = self.order.one_round_before(name, self.turn)
        if left is not None:
            self.pe.wait_ge(self.s.dve_taken if left[0] == "dve" else self.s.act_taken, left[1])
        return self.psum[:, self.order.bank(name), 0:n]

    def product(self, name, moving, n=T, ready=None, out=None, last=True):
        out = self.bank(name, n) if out is None else out
        for kc, rhs in enumerate(moving):
            if ready is not None:
                self.pe.wait_ge(ready[0], ready[1] + kc + 1)
            slot, i = divmod(self.k, SLOT_TILES)
            if i == 0:
                self.pe.wait_ge(self.s.slot_landed[slot % RING], (self.ring_turns + slot // RING + 1) * 16)
            mm = self.nc.tensor.matmul(out, self.ring[:, slot % RING, i * P:(i + 1) * P], rhs,
                                       start=(kc == 0), stop=(kc == len(moving) - 1))
            if kc == len(moving) - 1 and last:
                mm.then_inc(self.s.bank_full, 1)
            elif self.to_release:
                mm.then_inc(self.s.slot_used, self.to_release)
                self.to_release = 0
            self.k += 1
            self.to_release += i == SLOT_TILES - 1

    def finish(self, slots):
        used = -(-self.k // SLOT_TILES)
        for slot in range(used, slots):
            self.pe.wait_ge(self.s.slot_landed[slot % RING], (self.ring_turns + slot // RING + 1) * 16)
        left = self.to_release + (self.k % SLOT_TILES != 0) + slots - used
        if left:
            self.pe.drain().then_inc(self.s.slot_used, left)
        self.to_release = 0


def build(nc, weights, ada_in, x_in, p1_in, lam_in, const_in, ctx_in, p2_in, c_in, lora_in, lam_vec_in, out):
    s = Semaphores(nc)
    psum = nc.alloc_psum_tensor("psum", [P, BANKS, 512], F32)
    ring = nc.alloc_sbuf_tensor("ring", [P, RING, SLOT_TILES * P], F32)
    arena = nc.alloc_sbuf_tensor("arena", [P, 42900], F32)

    keep = Arena(arena)
    const = keep.take(C_COLS)

    def c_view(name):
        return const[:, C_AT[name]:C_AT[name] + CONST[name].shape[1]]

    p1 = keep.take(LAYERS * NP1)
    lam = keep.take(LAYERS * LH)
    final_gain = keep.take(DC)
    p2 = keep.take(NP2)
    c_vecs = keep.take(DC, 2)
    mod = keep.take(2, 3 * DC, 2)
    gain = keep.take(2, DC, 2)
    one_minus_ka = keep.take(DC)
    mean_of_d = keep.take(P)
    mean_of_head = keep.take(P)
    eps = keep.take(5)
    half_b = keep.take(4 * DC)
    s_state = keep.take(2, HEAD)
    p_end = keep.take(2, 2, STEPS)
    lam_vec = keep.take(4)
    lam_cols = keep.take(6)
    subln = keep.take(1)
    inv_count = c_view("inv_count").rearrange("p (g t) -> p g t", g=PG)

    first = Arena(arena, keep.at)
    x = first.take(DC, T)
    rms = first.take(T)
    rstd = first.take(T)
    xg = first.take(DC, T)
    sq = first.take(DC, T)
    second = Arena(arena, first.at)
    ta, tb, sa = first.take(2, T), first.take(2, T), first.take(2, T)
    u_pad = first.take(2, PAD + T)
    mixer = Arena(arena, first.at)
    hidden = first.take(FC, T)
    v = mixer.take(LH, T)
    i_gate, t_half, root, ge, hs = (mixer.take(LH, T) for _ in range(5))
    gl = mixer.take(2 * DC, T)
    pool_pad = mixer.take(PG, PAD + T)
    win_a, win_b = mixer.take(PAD + T), mixer.take(PAD + T)
    pooled, pool_out = mixer.take(PG, T), mixer.take(PG, T)
    y = mixer.take(DC, T)
    lt = mixer.take(6, LAYERS * LH)
    scr = mixer.take(4, T)
    ada = mixer.take(2, DC, P)
    ada_c = mixer.take(DC, P)
    ada_sums = mixer.take(MOD_CHUNKS, 2, P)
    mod_flat = mod.rearrange("p l m c -> p (l m c)")

    xx = second.take(DC, T2)
    rkv = second.take(3 * DC, T2)
    gate = second.take(DC, T2)
    lora_of = second.take(2, 2, T2)
    lora_w = second.take(2, PAIRS, P)
    x_at = keep.at
    h2 = Arena(arena, x_at + DC * T + 2 * T).take(DC, T2)
    sq2 = rkv[:, DC:2 * DC, :]
    on_x = Arena(arena, x_at)
    gram = on_x.take(2, 4, 2, P)
    on_h = Arena(arena, x_at + DC * T + 2 * T)
    w_dir, a_dir = on_h.take(2, T2), on_h.take(2, T2)
    o_dir = on_h.take(2, T2)
    kk_buf, kk_sq = on_h.take(T2), on_h.take(T2)
    on_ring = Arena(ring.rearrange("p a b -> p (a b)"))
    ar = on_ring.take(2, 2, STEPS, 2 * CHUNK)
    bk = on_ring.take(2, 2, STEPS, 2 * CHUNK)
    v_rev = on_ring.take(2, CHUNK + T2)
    prod = on_ring.take(STEPS, CHUNK + 1), second.take(STEPS, CHUNK + 1)
    norm_buf = second.take(T2)
    scan_at = second.at
    z_buf = second.take(1, P)
    on_counts = Arena(arena, C_AT["inv_count"])
    xi, t1 = on_counts.take(4, P), on_counts.take(4, P)
    ltm = second.take(4, P)
    yi = second.take(2, 4, P)
    shift_at = second.at
    bk_t = second.take(2, 4, P)
    uv = second.take(2, 4, P)
    kv_buf = (second.take(4 * HEAD), on_ring.take(4 * HEAD))
    lora_lo = Arena(arena, second.at).take(2, T2)
    ar_spread = second.take(2, 4, 2 * P)
    o_norm = second.take(T2)
    tmp = second.take(T2)
    tmp2 = Arena(arena, x_at + DC * T).take(T2)
    shift_pad = Arena(arena, shift_at).take(2, 2, T + 2)
    flat_v = rkv.rearrange("p a b -> p (a b)")

    k_all = rkv[:, 0:DC, :]
    v_tok = rkv[:, DC:2 * DC, :].rearrange("p h (c e) -> p h c e", c=4)
    q_all, g_all = (rkv[:, (4 + i) * 4:(5 + i) * 4, :].rearrange("p a b -> p (a b)").rearrange("p (h t) -> p h t", t=T)
                    for i in (0, 1))
    probs = gate[:, 0:4, :].rearrange("p (b c) t -> p b c t", b=2)
    probs_t = gate[:, 4:8, :].rearrange("p a b -> p (a b)").rearrange("p (b c t) -> p b c t", b=2, c=4)
    attn = Arena(arena, x_at).take(DA_HEADS, T)
    on_scan = Arena(arena, scan_at)
    squares, norms = on_scan.take(2, T2), on_scan.take(2, T2)
    v_feat = lora_of[:, 0, :, :]
    turned_sin = on_scan.take(T)
    maxima, sums = on_scan.take(2, 2), on_scan.take(2, 2)
    q_of = on_scan.take(2, DA_HEADS, T)
    assert on_scan.at <= second.at

    def p1_col(lay, name, i):
        return p1[:, bass.ds(lay * NP1 + P1[name] + i, 1)]

    def p2_col(name, i):
        return p2[:, P2[name] + i:P2[name] + i + 1]

    NRES = 3

    def streams(a):
        return a.rearrange("p (s t) -> p s t", s=2)

    def chunks(a, d):
        a = a.rearrange("p (s j t) -> p s j t", s=2, t=CHUNK)
        return a if d == 0 else a[:, :, ::-1, ::-1]

    def blocks(a):
        return a.rearrange("p (s j) t -> p s j t", s=2)

    def eng_is_vector(n, d):
        return n == 0 and d == 1

    def pairs_ready(n, d):
        return max(2 * n + d, 1)

    def direction(n, d, eng, tt, ts, link, t_):
        b = n % 2
        eng.wait_ge(s.products_ready, 2 * n + d + 1)
        if n >= 2:
            eng.wait_ge(s.os_full, STEPS * (n - 1))
        kk_, r_, k_ = (chunks(a, d) for a in (kk_buf, rkv[:, n, :], rkv[:, DC + n, :]))
        a_ = a_dir[:, d, :]
        a4, w4, t4 = (chunks(a, 0) for a in (a_, w_dir[:, d, :], t_))
        ar_, bk_ = ar[:, b, d, :, :], bk[:, b, d, :, :]
        link(ts(a_, a_, 0.5, 0.5, ALU.mult, ALU.add))
        tt(blocks(ar_[:, :, 0:CHUNK]), kk_, blocks(prod[d][:, :, 0:CHUNK]), ALU.mult)
        tt(blocks(ar_[:, :, CHUNK:]), r_, blocks(prod[d][:, :, 1:]), ALU.mult)
        link(tt(t4, kk_, a4, ALU.mult))
        link(tt(blocks(bk_[:, :, 0:CHUNK]), t4, w4, ALU.mult))
        link(ts(a_, a_, p2_col("ka", n), one_minus_ka[:, n:n + 1], ALU.mult, ALU.add))
        link(tt(t4, k_, a4, ALU.mult))
        done = s.first_backward_ready if eng_is_vector(n, d) else s.pair_ready
        tt(blocks(bk_[:, :, CHUNK:]), t4, w4, ALU.mult).then_inc(done, 1)
        if not eng_is_vector(n, d):
            eng.wait_ge(s.pair_ready, pairs_ready(n, d))


    ps_t1, ps_x, ps_y = ([psum[:, 3 + jj, i * 2 * P:(i + 1) * 2 * P].rearrange("p (u t) -> p u t", u=2)
                          for jj in range(2)] for i in (0, 0, 1))

    def half(tile, jj):
        return tile[:, 2 * jj:2 * jj + 2, :].rearrange("p u (b t) -> p (u b) t", t=CHUNK)

    def inverse_step(q, level, jj):
        before = q * (2 * LEVELS - 1) + 1
        return before if level == 0 else before + 2 * (level - 1) + jj + 1

    def masked_step(q, level, jj):
        return (q * (LEVELS - 1) + level - 1) * 2 + jj + 1

    with nc.Block() as block:

        @block.sync
        def _(sp):
            for dst, src in ((x, x_in), (p1, p1_in), (lam, lam_in[:, 0:LAYERS * LH]), (c_vecs, c_in)):
                sp.dma_start(dst, src).then_inc(s.loaded, 16)
            with sp.Fori(0, LAYERS * FIRST_SLOTS // RING) as turn:
                for r in range(RING):
                    sp.wait_ge(s.slot_used, turn * RING + r + 1)
                    sp.dma_start(ring[:, r, :], weights[turn * RING + r]).then_inc(s.slot_landed[r], 16)
            sp.wait_ge(s.bank_full, FIRST.full(("ffn2", "down", DC - 1), LAYERS - 1))
            for m in range(DC):
                sp.dma_start(xx[:, m, 0:T], ctx_in[:, m, :]).then_inc(s.context_loaded, 16)
            sp.dma_start(lora_w, lora_in).then_inc(s.context_loaded, 16)
            with sp.Fori(LAYERS * FIRST_SLOTS // RING, (LAYERS * FIRST_SLOTS + SECOND_A_SLOTS) // RING) as turn:
                for r in range(RING):
                    sp.wait_ge(s.slot_used, turn * RING + r + 1)
                    sp.dma_start(ring[:, r, :], weights[turn * RING + r]).then_inc(s.slot_landed[r], 16)
            sp.wait_ge(s.os_full, STEPS * PAIRS)
            before = LAYERS * FIRST_SLOTS + SECOND_A_SLOTS
            with sp.Fori(before // RING, (before + SECOND_B_SLOTS) // RING) as turn:
                for r in range(RING):
                    sp.wait_ge(s.slot_used, turn * RING + r + 1)
                    sp.dma_start(ring[:, r, :], weights[turn * RING + r]).then_inc(s.slot_landed[r], 16)
            for m in range(DC):
                sp.wait_ge(s.dve_taken, SECOND_B.taken(("da_out", m)))
                sp.dma_start(out[:, m, :], xx[:, m, T:]).then_inc(s.stored, 16)
            sp.wait_ge(s.stored, DC * 16)

        @block.tensor
        def _(pe):
            st = PeStream(nc, pe, ring, psum, s)
            pe.sem_inc(s.slot_used, RING)
            pe.wait_ge(s.tables_ready, 1)

            def mean_square(order_name, base):
                out_ = st.bank(order_name)
                for kc in range(DC):
                    pe.wait_ge(s.x_squared, base + kc + 1)
                    mm = nc.tensor.matmul(out_, mean_of_d, sq[:, kc, :], start=(kc == 0), stop=(kc == DC - 1))
                mm.then_inc(s.bank_full, 1)

            with pe.Fori(0, LAYERS) as lay:
                st.start(FIRST, lay)
                st.weights_from(lay * (FIRST_SLOTS // RING))
                xgs = [xg[:, kc, :] for kc in range(DC)]

                def modulation(i):
                    pe.wait_ge(s.mod_summed, (lay * 3 * DC + (i + 1) * MOD_CHUNKS) * 2)
                    out_ = st.bank(("mod", i), 2 * MOD_CHUNKS)
                    for k in range(2 * MOD_CHUNKS):
                        mm = nc.tensor.matmul(out_[:, k:k + 1], ada_sums[:, k // 2, k % 2, :], mean_of_d[:, 0:1],
                                              start=True, stop=True)
                    mm.then_inc(s.bank_full, 1)

                def feed_forward(ffn, no):
                    base = (lay * NRES + no) * DC
                    for j in range(FC):
                        st.product((ffn, "a", j), xgs, ready=(s.x_scaled, base) if j == 0 else None)
                        if j == 0:
                            mean_square((ffn, "mean_square"), base)
                        st.product((ffn, "b", j), xgs)
                        if j in MOD_AFTER:
                            modulation(MOD_AFTER.index(j) + (0 if ffn == "ffn1" else 4))
                    h_base = (lay * 2 + (no == 2)) * FC
                    for m in range(DC):
                        st.product((ffn, "down", m), [hidden[:, j, :] for j in range(FC)],
                                   ready=(s.hidden_written, h_base) if m == 0 else None)

                feed_forward("ffn1", 0)
                base = (lay * NRES + 1) * DC
                for h in range(LH):
                    st.product(("u_lru", h), xgs, ready=(s.x_scaled, base) if h == 0 else None)
                    if h == 0:
                        mean_square(("mix", "mean_square"), base)
                for g in range(PG):
                    st.product(("u_pool", g), xgs)
                for h in range(LH):
                    st.product(("u_gelu", h), xgs)
                for h in range(LH):
                    pe.wait_ge(s.conv_written, lay * LH + h + 1)
                    st.product(("gate_a", h), [v[:, h, :]])
                    st.product(("gate_x", h), [v[:, h, :]])
                for m in range(2 * DC):
                    st.product(("g_logit", m), xgs)
                    if m < PG:
                        pe.wait_ge(s.pooled_written, lay * PG + m + 1)
                        st.product(("pool_mix", m), [pooled[:, m, :]])
                modulation(2)
                for m in range(DC):
                    if m == 0:
                        pe.wait_ge(s.dve_taken, FIRST.taken(("pool_mix", PG - 1), lay))
                    st.product(("pool_up", m), [pool_out[:, g, :] for g in range(PG)])
                for m in range(DC):
                    st.product(("lru_up", m), [hs[:, h, :] for h in range(LH)],
                               ready=(s.lru_out_written, lay * LH) if m == 0 else None)
                modulation(3)
                for m in range(DC):
                    st.product(("w_out", m), [y[:, kc, :] for kc in range(DC)],
                               ready=(s.y_written, lay * DC) if m == 0 else None)
                feed_forward("ffn2", 2)
                assert st.k == FIRST_TILES
                st.finish(FIRST_SLOTS)

            st.start(SECOND_A)
            st.weights_from(LAYERS * FIRST_SLOTS // RING)
            st.all_banks_empty(SECOND_A)

            mean_square(("final", "mean_square"), LAYERS * NRES * DC)
            bank = st.bank(("rw", "mean_square"), T2)
            for kc in range(DC):
                pe.wait_ge(s.sq_ready, kc + 1)
                mm = nc.tensor.matmul(bank, mean_of_d, sq2[:, kc, :], start=(kc == 0), stop=(kc == DC - 1))
            mm.then_inc(s.bank_full, 1)
            for i, m in enumerate((4 * DC, 4 * DC + 1, *range(3 * DC), *range(3 * DC, 4 * DC))):
                st.product(("rw_in", m), [h2[:, kc, :] for kc in range(DC)], n=T2,
                           ready=(s.h_ready, 0) if i == 0 else None)
            assert st.k == SECOND_A_TILES
            st.finish(SECOND_A_SLOTS)

            st.start(SCAN)
            st.all_banks_empty(SCAN)
            same_head, identity = c_view("same_head"), c_view("identity")
            halves = (slice(0, HEAD), slice(HEAD, P))
            mm_ = nc.tensor.matmul
            gram_l, gram_lt = (psum[:, 0, i * 256:(i + 1) * 256].rearrange("p (u t) -> p u t", u=4) for i in (0, 1))
            gram_stack = psum[:, 1:3, :].rearrange("p b (u t) -> p (b u) t", u=2)
            ps_u = [psum[0:CHUNK, bank, at:at + P].rearrange("p (u t) -> p u t", u=2) for bank, at in U_BANKS]
            ps_z = psum[:, 5, 0:128].rearrange("p (u t) -> p u t", u=2)
            ps_o = psum[:, 5, 128:256].rearrange("p (u t) -> p u t", u=2)
            ps_s = psum[:, 2, 0:P].rearrange("p (u t) -> p u t", u=2)

            def turned(q):
                pair, g = divmod(q, GROUPS)
                b = pair % 2
                out_ = st.bank(("bk_turned", q), 512)
                for u in range(4):
                    jj, d = divmod(u, 2)
                    mm = nc.tensor.transpose(out_[:, u * P:(u + 1) * P], bk[:, b, d, 2 * g + jj, :], identity)
                mm.then_inc(s.bank_full, 1)
                out_ = st.bank(("v_turned", q), 512)
                for u in range(4):
                    jj, d = divmod(u, 2)
                    at = (2 * g + jj) * CHUNK
                    if d == 0:
                        at += (2 * DC + pair) * T2 - CHUNK
                        src = flat_v[:, at:at + 2 * CHUNK]
                    else:
                        src = v_rev[:, b, at:at + 2 * CHUNK]
                    mm = nc.tensor.transpose(out_[:, u * P:(u + 1) * P], src, identity)
                mm.then_inc(s.bank_full, 1)

            def side(q):
                pair, g = divmod(q, GROUPS)
                for name in scan_side_tiles(q):
                    kind, n = name[0], name[1]
                    if kind in ("bk_turned", "v_turned"):
                        continue
                    name = name[:-1]
                    out_ = st.bank(name, T2)
                    if kind == "kv":
                        pe.wait_ge(s.gram_taken, q + 1)
                        pe.wait_ge(s.act_taken, SCAN.taken(("v_turned", q)))
                        for u in range(4):
                            jj, d = divmod(u, 2)
                            for h in range(2):
                                mm = mm_(out_[halves[h], u * HEAD:(u + 1) * HEAD], gram_at(q % 2, jj, d, h)[HEAD:P, 0:CHUNK],
                                         uv[HEAD:P, q % 2, u, h * HEAD:(h + 1) * HEAD], start=True, stop=True)
                    elif kind == "kk_norm":
                        pe.wait_ge(s.kk_squared, n + 1)
                        mm = mm_(out_, same_head, kk_sq, start=True, stop=True)
                    elif kind in ("w", "a"):
                        i = 0 if kind == "w" else 1
                        mm = mm_(out_, lora_w[:, i, n, :], lora_of[:, i, name[2], :], start=True, stop=True)
                    elif kind == "o_mean":
                        pe.wait_ge(s.o_summed, n + 1)
                        mm = mm_(out_, mean_of_head, rkv[:, DC + n, :], start=True, stop=True)
                    elif kind == "o_var":
                        pe.wait_ge(s.o_squared, n + 1)
                        mm = mm_(out_, mean_of_head, kk_sq, start=True, stop=True)
                    elif kind == "bonus":
                        pe.wait_ge(s.bonus_in, n + 1)
                        mm = mm_(out_, same_head, tmp2, start=True, stop=True)
                    mm.then_inc(s.bank_full, 1)

            def scan_step(q, jj, stage):
                pair, g = divmod(q, GROUPS)
                b, par, step = pair % 2, q % 2, 2 * g + jj
                k = 2 * q + jj
                units = [(d, h) for d in range(2) for h in range(2)]
                if stage == "z":
                    pe.wait_ge(s.s_updated, k + 1)
                    if k >= 1:
                        pe.wait_ge(s.o_taken, k)
                    for d, h in units:
                        mm = mm_(ps_z[halves[h], d, :], ar[halves[h], b, d, step, 0:CHUNK], s_state[halves[h], d, :],
                                 start=True, stop=True)
                    mm.then_inc(s.z_full, 1)
                elif stage == "u":
                    pe.wait_ge(s.z_taken, k + 1)
                    for d, h in units:
                        mm = mm_(ps_u[h][:, d, :], yi[halves[h], par, 2 * jj + d, h * HEAD:(h + 1) * HEAD],
                                 z_buf[halves[h], 0, d * HEAD:(d + 1) * HEAD], start=True, stop=True)
                    mm.then_inc(s.u_full, 1)
                else:
                    pe.wait_ge(s.u_taken, k + 1)
                    for d, h in units:
                        cols = slice(h * HEAD, (h + 1) * HEAD)
                        o_ = ps_o[halves[h], d, :]
                        mm_(o_, s_state[halves[h], d, :], ar[halves[h], b, d, step, CHUNK:], start=True, stop=False)
                        mm_(o_, uv[:, par, 2 * jj + d, cols], gram_at(par, jj, d, h)[:, CHUNK:], start=False, stop=True)
                        mm = mm_(ps_s[halves[h], d, :], bk_t[:, par, 2 * jj + d, cols], uv[:, par, 2 * jj + d, cols],
                                 start=True, stop=True)
                    mm.then_inc(s.os_full, 1)

            def gram_at(par, jj, d, h):
                return gram[:, par, 2 * jj + d, h, :]

            for q in range(-GROUPS, 0):
                side(q)
            for q in range(PAIRS * GROUPS + 1):
                pieces = [(jj, stage) for jj in range(2) for stage in ("z", "u", "os")] if q >= 1 else []

                def piece(*place):
                    if pieces and place in STEP_PLACES:
                        scan_step(q - 1, *pieces[STEP_PLACES.index(place)])

                if q == PAIRS * GROUPS:
                    for stage in pieces:
                        scan_step(q - 1, *stage)
                    side(q)
                    break
                pair, g = divmod(q, GROUPS)
                b, par = pair % 2, q % 2
                if g == 0:
                    pe.wait_ge(s.pair_ready, pairs_ready(pair, 1))
                    if pair == 0:
                        pe.wait_ge(s.first_backward_ready, 1)
                    pe.wait_ge(s.reversed_ready, pair + 1)
                if q >= 1:
                    pe.wait_ge(s.gram_taken, q)
                    pe.wait_ge(s.s_updated, 2 * q - 1)
                for u in range(4):
                    jj, d = divmod(u, 2)
                    for h in range(2):
                        alpha = ar[halves[h], b, d, 2 * g + jj, 0:CHUNK]
                        beta = bk[halves[h], b, d, 2 * g + jj, 0:CHUNK]
                        mm_(gram_l[halves[h], u, :], alpha, beta, start=True, stop=True)
                        mm = mm_(gram_lt[halves[h], u, :], beta, alpha, start=True, stop=True)
                mm.then_inc(s.gram_full, 1)
                pe.wait_ge(s.spread_ready, q + 1)
                for u in range(4):
                    jj, d = divmod(u, 2)
                    mm = mm_(gram_stack[:, u, :], bk[:, b, d, 2 * g + jj, :], ar_spread[:, par, u, :], start=True, stop=True)
                mm.then_inc(s.stack_full, 1)
                turned(q)
                piece("start")
                for level in range(1, LEVELS):
                    for jj in range(2):
                        pe.wait_ge(s.xy_updated, inverse_step(q, level - 1, jj))
                        for u in (2 * jj, 2 * jj + 1):
                            mm = mm_(ps_t1[jj][:, u % 2, :], ltm[:, u, :], xi[:, u, :], start=True, stop=True)
                        mm.then_inc(s.t1_full, 1)
                    piece("t1", level)
                    for jj in range(2):
                        pe.wait_ge(s.t1_masked, masked_step(q, level, jj))
                        for u in (2 * jj, 2 * jj + 1):
                            y_, t_ = yi[:, par, u, :], t1[:, u, :]
                            mm = mm_(ps_y[jj][:, u % 2, :], t_, y_, start=True, stop=True)
                            if level < LEVELS - 1:
                                mm = mm_(ps_x[jj][:, u % 2, :], y_, t_, start=True, stop=True)
                        mm.then_inc(s.xy_full, 1)
                    piece("xy", level)
                side(q)
            for q in range(PAIRS * GROUPS + 1, (PAIRS + 1) * GROUPS):
                side(q)

            st.start(SECOND_B)
            st.weights_from((LAYERS * FIRST_SLOTS + SECOND_A_SLOTS) // RING)
            st.all_banks_empty(SECOND_B)
            for m in range(DC):
                st.product(("rw_out", m), [gate[:, kc, :] for kc in range(DC)], n=T2,
                           ready=(s.y_ready, 0) if m == 0 else None)
            bank = st.bank(("da", "mean_square"), T2)
            for kc in range(DC):
                pe.wait_ge(s.out_squared, kc + 1)
                mm = mm_(bank, mean_of_d, sq2[:, kc, :], start=(kc == 0), stop=(kc == DC - 1))
            mm.then_inc(s.bank_full, 1)
            for no, (kind, x_all, n) in enumerate((("k", k_all, T2), ("q", q_all, T))):
                for h in range(DA_HEADS + 2):
                    if h < DA_HEADS:
                        st.product((kind, h), [h2[:, kc, T2 - n:] for kc in range(DC)], n=n,
                                   ready=(s.h_ready, DC) if no == 0 and h == 0 else None)
                    if 1 <= h <= DA_HEADS:
                        pe.wait_ge(s.squared, no * DA_HEADS + h)
                        mm_(st.bank((kind + "_mean_square", h - 1), n), mean_of_head, squares[:, (h - 1) % 2, 0:n],
                            start=True, stop=True).then_inc(s.bank_full, 1)
                    if h >= 2:
                        pe.wait_ge(s.scaled, no * DA_HEADS + h - 1)
                        mm_(st.bank((kind + "_turned", h - 2)), c_view("rope_turn"), x_all[:, h - 2, n - T:],
                            start=True, stop=True).then_inc(s.bank_full, 1)
            for h in range(DA_HEADS + 1):
                if h < DA_HEADS:
                    st.product(("v", h), [h2[:, kc, :] for kc in range(DC)], n=T2)
                if h >= 1:
                    pe.wait_ge(s.act_taken, SECOND_B.taken(("v", h - 1)))
                    out_ = st.bank(("v_turned", h - 1), T2)
                    for c in range(4):
                        mm = nc.tensor.transpose(out_[:, c * P:(c + 1) * P], v_feat[:, (h - 1) % 2, c * P:(c + 1) * P],
                                                 identity)
                    mm.then_inc(s.bank_full, 1)
            for h in range(DA_HEADS):
                st.product(("g", h), [h2[:, kc, T:] for kc in range(DC)])
            pe.wait_ge(s.lam_in, 1)
            mm_(st.bank(("lam",), 2), mean_of_d[0:HEAD, :], lam_cols[0:HEAD, 0:2], start=True, stop=True)\
                .then_inc(s.bank_full, 1)
            pe.wait_ge(s.turned_in, 2 * DA_HEADS)
            for i in range(-1, 2 * DA_HEADS + 1):
                if i + 1 < 2 * DA_HEADS:
                    h, qb = divmod(i + 1, 2)
                    for c in range(2):
                        mm_(st.bank(("scores", i + 1, c), T2), q_of[:, c, h, qb * P:(qb + 1) * P],
                            k_all[:, h, :], start=True, stop=True).then_inc(s.bank_full, 1)
                if i >= 1:
                    pe.wait_ge(s.probs_ready, i)
                    out_ = st.bank(("probs_turned", i - 1), T2)
                    for c in range(4):
                        mm = nc.tensor.transpose(out_[:, c * P:(c + 1) * P], probs[:, (i - 1) % 2, 0, c * P:(c + 1) * P],
                                                 identity)
                    mm.then_inc(s.bank_full, 1)
                if i >= 2 and i % 2 == 0:
                    h = i // 2 - 1
                    pe.wait_ge(s.dve_taken, SECOND_B.taken(("probs_turned", 2 * h + 1)))
                    out_ = st.bank(("o", h))
                    for c in range(4):
                        mm = mm_(out_, v_tok[:, h, c, :], probs_t[:, h % 2, c, :], start=(c == 0), stop=(c == 3))
                    mm.then_inc(s.bank_full, 1)
            for h in range(DA_HEADS):
                pe.wait_ge(s.o_squared2, h + 1)
                mm_(st.bank(("o_mean_square", h)), mean_of_d, squares[:, h % 2, 0:T],
                    start=True, stop=True).then_inc(s.bank_full, 1)
            for m in range(DC):
                st.product(("da_out", m), [attn[:, h, :] for h in range(DA_HEADS)],
                           ready=(s.attn_ready, 0) if m == 0 else None)
            assert st.k == SECOND_B_TILES
            st.finish(SECOND_B_SLOTS)

        @block.scalar
        def _(act):
            act.sem_inc(s.act_taken, FIRST.count["act"])
            act.wait_ge(s.loaded, 4 * 16)
            act.wait_ge(s.tables_ready, 1)

            nc.scalar.activation(c_vecs, c_vecs, ACT.Silu).then_inc(s.c_silu, 1)

            act.wait_ge(s.log_done, 1)
            nc.scalar.activation(lt[:, 1, :], lt[:, 0, :], ACT.Exp, scale=-1.0).then_inc(s.log_done, 1)

            with act.Fori(0, LAYERS) as lay:

                def scale_and_square(name, updated_by, turn):
                    for m in range(DC):
                        act.wait_ge(s.dve_taken, FIRST.taken((*updated_by, m), turn))
                        nc.scalar.activation(xg[:, m, :], x[:, m, :], ACT.Copy,
                                             scale=p1_col(lay, name, m)).then_inc(s.x_scaled, 1)
                        nc.scalar.activation(sq[:, m, :], x[:, m, :], ACT.Square).then_inc(s.x_squared, 1)

                def root_mean_square(name, no):
                    act.wait_ge(s.bank_full, FIRST.full(name, lay))
                    nc.scalar.activation(rms, psum[:, FIRST.bank(name), 0:T], ACT.Sqrt,
                                         bias=eps[:, 0:1]).then_inc(s.act_taken, 1)

                def feed_forward(ffn, no):
                    if no == 0:
                        scale_and_square("norm_ffn1", ("ffn2", "down"), lay - 1)
                    else:
                        scale_and_square("norm_ffn2", ("w_out",), lay)
                    root_mean_square((ffn, "mean_square"), no)
                    f = lay * 2 + (no == 2)
                    for j in range(FC):
                        act.wait_ge(s.dve_taken, FIRST.taken((ffn, "a", j), lay))
                        nc.scalar.activation(sa[:, j % 2, :], ta[:, j % 2, :], ACT.Silu).then_inc(s.gate_silu, 1)

                feed_forward("ffn1", 0)
                scale_and_square("norm_mix", ("ffn1", "down"), lay)
                root_mean_square(("mix", "mean_square"), 1)
                for h in range(LH):
                    act.wait_ge(s.dve_taken, FIRST.taken(("u_gelu", h), lay))
                    nc.scalar.activation(ge[:, h, :], ge[:, h, :], ACT.Gelu_apprx_tanh).then_inc(s.gelu_done, 1)
                for h in range(LH):
                    for name, dst, b in (("gate_a", t_half, "b_a"), ("gate_x", i_gate, "b_x")):
                        act.wait_ge(s.bank_full, FIRST.full((name, h), lay))
                        nc.scalar.activation(dst[:, h, :], psum[:, FIRST.bank((name, h)), 0:T], ACT.Sigmoid,
                                             bias=p1_col(lay, b, h)).then_inc(s.act_taken, 1)
                for h in range(LH):
                    act.wait_ge(s.act_taken, FIRST.taken(("gate_x", h), lay))
                    nc.scalar.activation(t_half[:, h, :], t_half[:, h, :], ACT.Tanh,
                                         scale=lam[:, bass.ds(lay * LH + h, 1)]).then_inc(s.lru_tanh_done, 1)
                for h in range(LH):
                    act.wait_ge(s.lru_tanh_done, lay * LH + h + 1)
                    nc.scalar.activation(root[:, h, :], t_half[:, h, :], ACT.Sqrt).then_inc(s.lru_root_done, 1)
                for m in range(2 * DC):
                    act.wait_ge(s.dve_taken, FIRST.taken(("g_logit", m), lay))
                    nc.scalar.activation(gl[:, m, :], gl[:, m, :], ACT.Sigmoid).then_inc(s.g_done, 1)
                feed_forward("ffn2", 2)

            for m in range(DC):
                act.wait_ge(s.dve_taken, FIRST.taken(("ffn2", "down", m), LAYERS - 1))
                nc.scalar.activation(sq[:, m, :], x[:, m, :], ACT.Square).then_inc(s.x_squared, 1)
            name = ("final", "mean_square")
            act.wait_ge(s.bank_full, SECOND_A.full(name))
            nc.scalar.activation(rms, psum[:, SECOND_A.bank(name), 0:T], ACT.Sqrt, bias=eps[:, 0:1]).then_inc(s.act_taken, 1)
            act.wait_ge(s.context_loaded, 9 * 16)
            for m in range(DC):
                act.wait_ge(s.x_normed, m + 1)
                nc.scalar.activation(sq2[:, m, :], xx[:, m, :], ACT.Square).then_inc(s.sq_ready, 1)
            name = ("rw", "mean_square")
            act.wait_ge(s.bank_full, SECOND_A.full(name))
            nc.scalar.activation(norm_buf, psum[:, SECOND_A.bank(name), :], ACT.Sqrt, bias=eps[:, 0:1]).then_inc(s.act_taken, 1)
            for i, m in enumerate((4 * DC, 4 * DC + 1, *range(3 * DC))):
                act.wait_ge(s.bank_full, SECOND_A.full(("rw_in", m)))
                if i >= 2:
                    act.wait_ge(s.mixed, i - 1)
                nc.scalar.activation(shift_pad[:, i % 2, :, 1:T + 1],
                                     psum[:, SECOND_A.bank(("rw_in", m)), :].rearrange("p (s t) -> p s t", s=2),
                                     ACT.Copy).then_inc(s.act_taken, 1)
            for i in range(2):
                act.wait_ge(s.mixed, i + 1)
                for d, rows in enumerate((slice(0, HEAD), slice(HEAD, P))):
                    nc.scalar.activation(lora_of[rows, i, d, :], lora_lo[rows, i, :],
                                         ACT.Copy if i else ACT.Tanh).then_inc(s.lora_in, 1)
            for m in range(3 * DC, 4 * DC):
                act.wait_ge(s.bank_full, SECOND_A.full(("rw_in", m)))
                nc.scalar.activation(gate[:, m - 3 * DC, :], psum[:, SECOND_A.bank(("rw_in", m)), :],
                                     ACT.Silu).then_inc(s.act_taken, 1)

            def scan_tile(*name):
                act.wait_ge(s.bank_full, SCAN.full(name))
                return psum[:, SCAN.bank(name), :]

            def side_head(q):
                pair, g = divmod(q, GROUPS)
                n = pair + 1
                if g == 0 and n < PAIRS:
                    act.wait_ge(s.kk_scaled, n + 1)
                    nc.scalar.activation(kk_sq, kk_buf, ACT.Square).then_inc(s.kk_squared, 1)
                    if n == 0:
                        act.wait_ge(s.mixed, 3 * DC + 2)
                    nc.scalar.activation(v_rev[:, n % 2, CHUNK:].rearrange("p (s t) -> p s t", s=2),
                                         rkv[:, 2 * DC + n, :].rearrange("p (s t) -> p s t", s=2)[:, :, ::-1],
                                         ACT.Copy).then_inc(s.reversed_ready, 1)
                if g == 2 and pair >= 1:
                    act.wait_ge(s.dve_taken, SCAN.taken(("o_mean", pair - 1)))
                    nc.scalar.activation(kk_sq, rkv[:, DC + pair - 1, :], ACT.Square).then_inc(s.o_squared, 1)

            def side_tail(q):
                for *name, by in scan_side_tiles(q):
                    kind, n = name[0], name[1]
                    if by != "act" or kind in ("bk_turned", "v_turned"):
                        continue
                    src = scan_tile(*name)
                    if kind == "kk_norm":
                        nc.scalar.activation(norm_buf, src, ACT.Sqrt, bias=eps[:, 1:2]).then_inc(s.act_taken, 1)
                    elif kind == "kv":
                        nc.scalar.activation(kv_buf[q % 2], src[:, 0:4 * HEAD], ACT.Copy).then_inc(s.act_taken, 1)
                    elif kind == "o_var":
                        if n >= 1:
                            act.wait_ge(s.y_ready, n)
                        nc.scalar.activation(o_norm, src, ACT.Sqrt, bias=eps[:, 2:3]).then_inc(s.act_taken, 1)
                    else:
                        d = name[2]
                        src = src.rearrange("p (s t) -> p s t", s=2)
                        if d == 1:
                            src = src[:, :, ::-1]
                        i, dst = (0, w_dir) if kind == "w" else (1, a_dir)
                        if kind == "w" and d == 0 and n >= 1:
                            act.wait_ge(s.bonus_in, n)
                        at = (2 * i + d) * DC + n
                        nc.scalar.activation(dst[:, d, :].rearrange("p (s t) -> p s t", s=2), src, ACT.Tanh,
                                             scale=0.5, bias=half_b[:, at:at + 1]).then_inc(s.act_taken, 1)
                        if kind == "a":
                            act.wait_ge(s.act_taken, SCAN.taken(("w", n, d)))
                            nc.scalar.activation(w_dir[:, d, :], w_dir[:, d, :], ACT.Exp,
                                                 scale=-DECAY / 2, bias=eps[:, 4:5]).then_inc(s.wa_ready, 1)

            act.wait_ge(s.slot_used, RING_AT_REST)
            for q in range(-GROUPS, 0):
                side_head(q)
                side_tail(q)
            for q in range((PAIRS + 1) * GROUPS):
                pair, g = divmod(q, GROUPS)
                par = q % 2
                side_head(q)
                if q < PAIRS * GROUPS:
                    src = scan_tile("bk_turned", q)
                    nc.scalar.activation(bk_t[:, par, :, :], src.rearrange("p (u t) -> p u t", u=4),
                                         ACT.Copy).then_inc(s.act_taken, 1)
                    src = scan_tile("v_turned", q)
                    nc.scalar.activation(uv[CHUNK:P, par, :, :], src[CHUNK:P, :].rearrange("p (u t) -> p u t", u=4),
                                         ACT.Copy).then_inc(s.act_taken, 1)
                if 1 <= q <= PAIRS * GROUPS:
                    was_pair, was_g = divmod(q - 1, GROUPS)
                    for jj in range(2):
                        k = 2 * (q - 1) + jj
                        act.wait_ge(s.u_full, k + 1)
                        for h, (bank, at) in enumerate(U_BANKS):
                            ins = nc.scalar.activation(
                                uv[0:CHUNK, (q - 1) % 2, 2 * jj:2 * jj + 2, h * HEAD:(h + 1) * HEAD],
                                psum[0:CHUNK, bank, at:at + P].rearrange("p (u t) -> p u t", u=2), ACT.Copy, scale=-1.0)
                        ins.then_inc(s.u_taken, 1)
                        act.wait_ge(s.os_full, k + 1)
                        if was_g == 0 and jj == 0 and was_pair >= 1:
                            act.wait_ge(s.o_summed, was_pair)
                        at = (2 * was_g + jj) * CHUNK
                        nc.scalar.activation(o_dir[:, :, at:at + CHUNK],
                                             psum[:, 5, 128:256].rearrange("p (u t) -> p u t", u=2),
                                             ACT.Copy).then_inc(s.o_taken, 1)
                side_tail(q)

            def tile_b(*name, n=T2):
                act.wait_ge(s.bank_full, SECOND_B.full(name))
                return psum[:, SECOND_B.bank(name), 0:n]

            for m in range(DC):
                act.wait_ge(s.dve_taken, SECOND_B.taken(("rw_out", m)))
                nc.scalar.activation(sq2[:, m, :], xx[:, m, :], ACT.Square).then_inc(s.out_squared, 1)
            nc.scalar.activation(norm_buf, tile_b("da", "mean_square"), ACT.Sqrt, bias=eps[:, 0:1]).then_inc(s.act_taken, 1)
            for no, (kind, x_all, n) in enumerate((("k", k_all, T2), ("q", q_all, T))):
                for h in range(DA_HEADS + 1):
                    if h < DA_HEADS:
                        src = tile_b(kind, h, n=n)
                        nc.scalar.activation(squares[:, h % 2, 0:n], src, ACT.Square).then_inc(s.squared, 1)
                        nc.scalar.activation(x_all[:, h, :], src, ACT.Copy).then_inc(s.act_taken, 1)
                    if h >= 1:
                        src = tile_b(kind + "_mean_square", h - 1, n=n)
                        if no * DA_HEADS + h > 2:
                            act.wait_ge(s.scaled, no * DA_HEADS + h - 2)
                        nc.scalar.activation(norms[:, (h - 1) % 2, 0:n], src, ACT.Sqrt,
                                             bias=eps[:, 0:1]).then_inc(s.act_taken, 1)
            for h in range(DA_HEADS + 1):
                if h < DA_HEADS:
                    nc.scalar.activation(v_feat[:, h % 2, :], tile_b("v", h), ACT.Copy).then_inc(s.act_taken, 1)
                if h >= 1:
                    nc.scalar.activation(v_tok[:, h - 1, :, :],
                                         tile_b("v_turned", h - 1).rearrange("p (c e) -> p c e", c=4),
                                         ACT.Copy).then_inc(s.act_taken, 1)
            for h in range(DA_HEADS):
                nc.scalar.activation(g_all[:, h, :], tile_b("g", h, n=T), ACT.Silu).then_inc(s.act_taken, 1)
            nc.scalar.activation(lam_cols[:, 2:4], tile_b("lam", n=2), ACT.Exp, scale=float(D)).then_inc(s.act_taken, 1)
            for i in range(2 * DA_HEADS):
                act.wait_ge(s.max_ready, i + 1)
                for c in range(2):
                    nc.scalar.activation(probs[:, i % 2, c, :], tile_b("scores", i, c), ACT.Exp,
                                         bias=maxima[:, i % 2, c:c + 1], scale=SCALE,
                                         accum_out=sums[:, i % 2, c:c + 1]).then_inc(s.act_taken, 1)
            for i in range(DA_HEADS + 1):
                if i < DA_HEADS:
                    act.wait_ge(s.dve_taken, SECOND_B.taken(("o", i)))
                    nc.scalar.activation(squares[:, i % 2, 0:T], attn[:, i, :], ACT.Square).then_inc(s.o_squared2, 1)
                if i >= 1:
                    h = i - 1
                    if h >= 2:
                        act.wait_ge(s.attn_ready, h - 1)
                    nc.scalar.activation(norms[:, h % 2, 0:T], tile_b("o_mean_square", h, n=T), ACT.Sqrt,
                                         bias=eps[:, 3:4], scale=float(D // P)).then_inc(s.act_taken, 1)

        @block.gpsimd
        def _(pool):
            tt, ts = nc.gpsimd.tensor_tensor, nc.gpsimd.tensor_scalar
            link = Chain(pool, s.pool_chain)

            pool.wait_ge(s.slot_landed[0], 16)
            for dst, src in ((const, const_in), (p2, p2_in), (final_gain, lam_in[:, LAYERS * LH:]),
                             (lam_vec[0:HEAD, :], lam_vec_in)):
                pool.dma_start(dst, src).then_inc(s.tables_loaded, 16)
            pool.wait_ge(s.loaded, 4 * 16)
            pool.wait_ge(s.c_silu, 1)
            with pool.Fori(0, LAYERS) as lay:
                for m in range(3 * DC):
                    for ahead in ((0, 1) if m == 0 else (1,)):
                        if m + ahead < 3 * DC:
                            pool.dma_start(ada[:, (m + ahead) % 2, :, :], ada_in[lay * 3 * DC + m + ahead])\
                                .then_inc(s.mod_landed[(m + ahead) % 2], 16)
                    pool.wait_ge(s.mod_landed[m % 2], (lay * (3 * DC // 2) + m // 2 + 1) * 16)
                    i, k = divmod(m, MOD_CHUNKS)
                    if k == 0:
                        pool.wait_ge(s.dve_taken, FIRST.taken(("mod", (i - 1) % MOD_TILES), lay - 1 if i == 0 else lay))
                    for c in range(2):
                        step = ((lay * 3 * DC + m) * 2 + c) * 3
                        for n, (dst, a_, b_) in enumerate((
                                (ada_c, ada[:, m % 2, :, :], c_vecs[:, :, c].unsqueeze(2).to_broadcast([P, DC, P])),
                                (ada_c[:, 0:4, :], ada_c[:, 0:4, :], ada_c[:, 4:8, :]),
                                (ada_c[:, 0:2, :], ada_c[:, 0:2, :], ada_c[:, 2:4, :]))):
                            tt(dst, a_, b_, ALU.add if n else ALU.mult).then_inc(s.mod_product, 1)
                            pool.wait_ge(s.mod_product, step + n + 1)
                        tt(ada_sums[:, k, c, :], ada_c[:, 0, :], ada_c[:, 1, :], ALU.add).then_inc(s.mod_summed, 1)
                        pool.wait_ge(s.mod_summed, (lay * 3 * DC + m) * 2 + c + 1)

            pool.wait_ge(s.slot_used, RING_AT_REST)
            pool.wait_ge(s.mixed, 3 * DC + 2)
            pool.wait_ge(s.lora_in, 4)

            def spread(q):
                pair, g = divmod(q, GROUPS)
                if q >= 2:
                    pool.wait_ge(s.stack_full, q - 1)
                for h in range(2):
                    dst = ar_spread[:, q % 2, :, h * P:(h + 1) * P].rearrange("p (j d) t -> p d j t", d=2)
                    ins = ts(dst, ar[:, pair % 2, :, 2 * g:2 * g + 2, :], c_view("same_head")[:, h * HEAD:h * HEAD + 1],
                             None, ALU.mult)
                ins.then_inc(s.spread_ready, 1)

            for q in range(-GROUPS, (PAIRS + 1) * GROUPS):
                pair, g = divmod(q, GROUPS)
                n, was = pair + 1, pair - 1
                ahead, behind = n < PAIRS, was >= 0
                if -1 <= q < PAIRS * GROUPS - 1:
                    if q == -1:
                        pool.wait_ge(s.first_backward_ready, 1)
                    spread(q + 1)
                if g == 0 and ahead:
                    ts(kk_buf, rkv[:, DC + n, :], p2_col("kk", n), None, ALU.mult).then_inc(s.kk_scaled, 1)
                if g == 1:
                    if behind:
                        pool.wait_ge(s.o_taken, STEPS * (was + 1))
                        tt(streams(rkv[:, DC + was, :]), streams(o_dir[:, 0, :]), streams(o_dir[:, 1, :])[:, :, ::-1],
                           ALU.add).then_inc(s.o_summed, 1)
                    if ahead:
                        pool.wait_ge(s.kk_inverse, n + 1)
                        tt(kk_buf, kk_buf, norm_buf, ALU.mult).then_inc(s.kk_normed, 1)
                        pool.wait_ge(s.kk_normed, n + 1)
                        direction(n, 0, pool, tt, ts, link, tmp)
                if g == 2 and n >= 1 and ahead:
                    direction(n, 1, pool, tt, ts, link, tmp)
                if g == 3:
                    if behind:
                        o_ = rkv[:, DC + was, :]
                        pool.wait_ge(s.o_inverse, was + 1)
                        link(tt(o_, o_, o_norm, ALU.mult))
                        link(ts(o_, o_, p2_col("gn_g", was), p2_col("gn_b", was), ALU.mult, ALU.add))
                        link(tt(o_, o_, rkv[:, was, :], ALU.add))
                        tt(gate[:, was, :], o_, gate[:, was, :], ALU.mult).then_inc(s.y_ready, 1)
                    if ahead:
                        link(tt(streams(tmp), streams(a_dir[:, 0, :]), streams(a_dir[:, 1, :])[:, :, ::-1], ALU.add))
                        link(ts(tmp, tmp, p2_col("rk", n), None, ALU.mult))
                        link(tt(tmp, tmp, rkv[:, n, :], ALU.mult))
                        if n >= 1:
                            pool.wait_ge(s.dve_taken, SCAN.taken(("bonus", n - 1)))
                        tt(tmp2, tmp, rkv[:, DC + n, :], ALU.mult).then_inc(s.bonus_in, 1)

            pool.wait_ge(s.dve_taken, SECOND_B.taken(("rw_out", DC - 1)))
            nc.gpsimd.memset(q_of, 0.0).then_inc(s.q_zeroed, 1)

        @block.vector
        def _(dve):
            tt, ts, stt = nc.vector.tensor_tensor, nc.vector.tensor_scalar, nc.vector.scalar_tensor_tensor
            link = Chain(dve, s.dve_chain)
            dve.sem_inc(s.dve_taken, FIRST.count["dve"])
            nc.vector.memset(mean_of_d, 1.0 / D)
            nc.vector.memset(eps[:, 0:1], EPS)
            nc.vector.memset(eps[:, 1:2], 1e-12)
            nc.vector.memset(eps[:, 2:3], GN_EPS)
            nc.vector.memset(eps[:, 3:4], SUBLN_EPS)
            nc.vector.memset(eps[:, 4:5], -DECAY / 2)
            nc.vector.memset(u_pad[:, :, 0:PAD], 0.0)
            link(nc.vector.memset(pool_pad[:, :, 0:PAD], 0.0))
            link(nc.vector.memset(win_a, 0.0))
            nc.vector.memset(win_b, 0.0).then_inc(s.tables_ready, 1)
            dve.wait_ge(s.loaded, 4 * 16)

            link(ts(lt[:, 2, :], lam, -1.0, None, ALU.mult))
            tt(lt[:, 0, :], lam, lt[:, 2, :], ALU.max).then_inc(s.log_done, 1)
            dve.wait_ge(s.log_done, 2)
            e, z, z2, acc = lt[:, 1, :], lt[:, 3, :], lt[:, 4, :], lt[:, 5, :]
            link(ts(z, e, 2.0, None, ALU.add))
            link(nc.vector.reciprocal(z2, z))
            link(tt(z, e, z2, ALU.mult))
            link(tt(z2, z, z, ALU.mult))
            link(ts(acc, z2, 1.0 / 17, 1.0 / 15, ALU.mult, ALU.add))
            for k in (13, 11, 9, 7, 5, 3, 1):
                link(tt(acc, acc, z2, ALU.mult))
                link(ts(acc, acc, 1.0 / k, None, ALU.add))
            link(tt(acc, acc, z, ALU.mult))
            link(ts(lt[:, 2, :], lt[:, 2, :], 0.0, None, ALU.max))
            link(stt(acc, acc, 2.0, lt[:, 2, :], ALU.mult, ALU.add))
            link(ts(lam, acc, LRU_C / 2, None, ALU.mult))
            before_layers = link.n
            dve.wait_ge(s.tables_loaded, 4 * 16)

            with dve.Fori(0, LAYERS) as lay:
                link.start(lay * FIRST_STEPS + before_layers)

                def full(name):
                    dve.wait_ge(s.bank_full, FIRST.full(name, lay))
                    return psum[:, FIRST.bank(name), 0:T]

                def take(ins, name, wait=True):
                    ins.then_inc(s.dve_taken, 1)
                    if wait:
                        dve.wait_ge(s.dve_taken, FIRST.taken(name, lay))

                def inverse_rms(name):
                    dve.wait_ge(s.act_taken, FIRST.taken(name, lay))
                    link(nc.vector.reciprocal(rstd, rms))

                def modulation(i):
                    name, n = ("mod", i), 2 * MOD_CHUNKS
                    src = full(name)[:, 0:n].rearrange("p (m c) -> p m c", c=2)
                    dst = mod_flat[:, bass.ds(lay * 6 * DC + i * n, n)].rearrange("p (m c) -> p m c", c=2)
                    bias = p2[:, bass.ds(lay * 3 * DC + P2["ada_b"] + i * MOD_CHUNKS, MOD_CHUNKS)]
                    take(stt(dst, src, float(D), bias.unsqueeze(2).to_broadcast([P, MOD_CHUNKS, 2]), ALU.mult, ALU.add),
                         name, wait=False)

                def feed_forward(ffn, no):
                    f = lay * 2 + (no == 2)
                    inverse_rms((ffn, "mean_square"))
                    for j in range(FC):
                        b = j % 2
                        take(tt(ta[:, b, :], full((ffn, "a", j)), rstd, ALU.mult), (ffn, "a", j), wait=False)
                        take(tt(tb[:, b, :], full((ffn, "b", j)), rstd, ALU.mult), (ffn, "b", j))
                        dve.wait_ge(s.gate_silu, f * FC + j + 1)
                        tt(hidden[:, j, :], tb[:, b, :], sa[:, b, :], ALU.mult).then_inc(s.hidden_written, 1)
                        if j in MOD_AFTER:
                            modulation(MOD_AFTER.index(j) + (0 if ffn == "ffn1" else 4))
                    for m in range(DC):
                        name = (ffn, "down", m)
                        take(stt(x[:, m, :], full(name), 0.5, x[:, m, :], ALU.mult, ALU.add), name, wait=False)

                feed_forward("ffn1", 0)
                inverse_rms(("mix", "mean_square"))
                for h in range(LH):
                    u = u_pad[:, h % 2, :]
                    take(tt(u[:, PAD:], full(("u_lru", h)), rstd, ALU.mult), ("u_lru", h))
                    first_tap = PAD - CONV + 1
                    link(ts(v[:, h, :], u[:, first_tap:first_tap + T], p1_col(lay, "conv_w", h),
                            p1_col(lay, "conv_b", h), ALU.mult, ALU.add))
                    for k in range(1, CONV):
                        ins = stt(v[:, h, :], u[:, first_tap + k:first_tap + k + T],
                                  p1_col(lay, "conv_w", k * LH + h), v[:, h, :], ALU.mult, ALU.add)
                        if k < CONV - 1:
                            link(ins)
                    ins.then_inc(s.conv_written, 1)
                dve.wait_ge(s.conv_written, lay * LH + LH)
                for g in range(PG):
                    u = pool_pad[:, g, :]
                    take(tt(u[:, PAD:], full(("u_pool", g)), rstd, ALU.mult), ("u_pool", g))
                    prev, step = u, 1
                    for i in range(g + 1):
                        dst = (win_a, win_b)[i % 2]
                        link(tt(dst[:, step:], prev[:, step:], prev[:, 0:PAD + T - step], ALU.add))
                        prev, step = dst, 2 * step
                    assert step == WINDOWS[g]
                    link(tt(scr[:, 0, :], prev[:, PAD:], inv_count[:, g, :], ALU.mult))
                    tt(pooled[:, g, :], scr[:, 0, :], u[:, PAD:], ALU.subtract).then_inc(s.pooled_written, 1)
                    dve.wait_ge(s.pooled_written, lay * PG + g + 1)
                for h in range(LH):
                    take(tt(ge[:, h, :], full(("u_gelu", h)), rstd, ALU.mult), ("u_gelu", h), wait=False)

                def g_logits(m):
                    take(tt(gl[:, m, :], full(("g_logit", m)), rstd, ALU.mult), ("g_logit", m), wait=False)
                    if m < PG:
                        take(ts(pool_out[:, m, :], full(("pool_mix", m)), p1_col(lay, "pool_b", m),
                                p1_col(lay, "pool_scale", m), ALU.add, ALU.mult), ("pool_mix", m), wait=False)

                def recurrence(h):
                    t = t_half[:, h, :]
                    dve.wait_ge(s.lru_root_done, lay * LH + h + 1)
                    link(ts(scr[:, 0, :], t, 1.0, None, ALU.add))
                    link(nc.vector.reciprocal(scr[:, 1, :], scr[:, 0, :]))
                    ts(scr[:, 2, :], scr[:, 1, :], 2.0, -1.0, ALU.mult, ALU.add)
                    link(tt(scr[:, 3, :], i_gate[:, h, :], v[:, h, :], ALU.mult))
                    link(stt(scr[:, 1, :], root[:, h, :], 2.0, scr[:, 1, :], ALU.mult, ALU.mult))
                    link(tt(scr[:, 1, :], scr[:, 1, :], scr[:, 3, :], ALU.mult))
                    link(nc.vector.tensor_tensor_scan(hs[:, h, :], scr[:, 2, :], scr[:, 1, :], 0.0, ALU.mult, ALU.add))
                    dve.wait_ge(s.gelu_done, lay * LH + h + 1)
                    tt(hs[:, h, :], hs[:, h, :], ge[:, h, :], ALU.mult).then_inc(s.lru_out_written, 1)
                    dve.wait_ge(s.lru_out_written, lay * LH + h + 1)

                for m in range(2 * DC):
                    g_logits(m)
                    if m < LH:
                        recurrence(m)
                modulation(2)
                for m in range(DC):
                    dve.wait_ge(s.g_done, lay * 2 * DC + m + 1)
                    take(tt(y[:, m, :], full(("pool_up", m)), gl[:, m, :], ALU.mult), ("pool_up", m), wait=m == DC - 1)
                for m in range(DC):
                    dve.wait_ge(s.g_done, lay * 2 * DC + DC + m + 1)
                    take(tt(scr[:, m % 2, :], full(("lru_up", m)), gl[:, DC + m, :], ALU.mult), ("lru_up", m))
                    tt(y[:, m, :], scr[:, m % 2, :], y[:, m, :], ALU.add).then_inc(s.y_written, 1)
                modulation(3)
                for m in range(DC):
                    take(tt(x[:, m, :], full(("w_out", m)), x[:, m, :], ALU.add), ("w_out", m), wait=False)
                feed_forward("ffn2", 2)
                assert link.n == FIRST_STEPS, link.n

            link.start(before_layers + LAYERS * FIRST_STEPS)

            def full2(order, name, n=T2):
                dve.wait_ge(s.bank_full, order.full(name))
                return psum[:, order.bank(name), 0:n]

            def take2(order, ins, name, wait=True):
                ins.then_inc(s.dve_taken, 1)
                if wait:
                    dve.wait_ge(s.dve_taken, order.taken(name))

            dve.wait_ge(s.dve_taken, FIRST.taken(("mod", MOD_TILES - 1), LAYERS - 1))
            for layer in range(2):
                g_ = p2[:, P2["norm_g"] + layer * DC:P2["norm_g"] + (layer + 1) * DC]
                link(ts(gain[:, layer, :, :], mod[:, layer, DC:2 * DC, :], 1.0, None, ALU.add))
                link(tt(gain[:, layer, :, :], gain[:, layer, :, :], g_.unsqueeze(2).to_broadcast([P, DC, 2]), ALU.mult))
            dve.wait_ge(s.act_taken, SECOND_A.taken(("final", "mean_square")))
            link(nc.vector.reciprocal(rstd, rms))
            for m in range(DC):
                stt(xx[:, m, T:], x[:, m, :], final_gain[:, m:m + 1], rstd, ALU.mult, ALU.mult).then_inc(s.x_normed, 1)
            ka = p2[:, P2["ka"]:P2["ka"] + DC]
            link(ts(one_minus_ka, ka, -1.0, 1.0, ALU.mult, ALU.add))
            link(ts(half_b, p2[:, P2["w0"]:P2["w0"] + 4 * DC], 0.5, None, ALU.mult))
            link(ts(mean_of_head, c_view("same_head"), 1.0 / HEAD, None, ALU.mult))

            def modulated_norm(layer, order, name):
                dve.wait_ge(s.act_taken, order.taken(name))
                link(nc.vector.reciprocal(norm_buf, norm_buf))
                for m in range(DC):
                    for c in range(2):
                        part = slice(c * T, (c + 1) * T)
                        link(stt(h2[:, m, part], xx[:, m, part], gain[:, layer, m, c:c + 1], norm_buf[:, part],
                                 ALU.mult, ALU.mult))
                        ins = ts(h2[:, m, part], h2[:, m, part], mod[:, layer, m, c:c + 1], None, ALU.add)
                    ins.then_inc(s.h_ready, 1)

            link(nc.vector.memset(lora_of, 0.0))
            link(nc.vector.memset(shift_pad, 0.0))
            modulated_norm(0, SECOND_A, ("rw", "mean_square"))
            for i, m in enumerate((4 * DC, 4 * DC + 1, *range(3 * DC))):
                dve.wait_ge(s.act_taken, SECOND_A.taken(("rw_in", m)))
                u = shift_pad[:, i % 2, :, :]
                here = u[:, :, 1:T + 1]
                dst = (lora_lo[:, i, :] if i < 2 else rkv[:, m, :]).rearrange("p (s t) -> p s t", s=2)
                t_ = tmp.rearrange("p (s t) -> p s t", s=2)
                link(tt(t_, u[:, :, 0:T], u[:, :, 2:T + 2], ALU.add))
                link(stt(t_, t_, 0.5, here, ALU.mult, ALU.subtract))
                stt(dst, t_, p2_col("mu", m - DC if m >= 4 * DC else m), here, ALU.mult, ALU.add).then_inc(s.mixed, 1)
                dve.wait_ge(s.mixed, i + 1)

            dve.wait_ge(s.slot_used, RING_AT_REST)
            for one in prod:
                link(nc.vector.memset(one[:, :, 0:1], 1.0))
            link(nc.vector.memset(v_rev[:, :, 0:CHUNK], 0.0))
            for zeros in (xi, ltm, yi):
                link(nc.vector.memset(zeros, 0.0))
            nc.vector.memset(s_state, 0.0).then_inc(s.s_updated, 1)

            def inverse(a, by):
                for i in range(4):
                    ins = nc.vector.reciprocal(a[:, i * P:(i + 1) * P], a[:, i * P:(i + 1) * P])
                    if i < 3:
                        yield
                ins.then_inc(by, 1)

            def side(q):
                pair, g = divmod(q, GROUPS)
                n, was = pair + 1, pair - 1
                if g == 1 and n < PAIRS:
                    dve.wait_ge(s.act_taken, SCAN.taken(("kk_norm", n)))
                    yield from inverse(norm_buf, s.kk_inverse)
                if g in (1, 2) and n < PAIRS:
                    d = g - 1
                    dve.wait_ge(s.wa_ready, 2 * n + d + 1)
                    w_ = w_dir[:, d, :]
                    for j in range(STEPS):
                        part = w_[:, j * CHUNK:(j + 1) * CHUNK]
                        ins = nc.vector.tensor_tensor_scan(prod[d][:, j, 1:], part, part, 1.0, ALU.mult, ALU.bypass)
                        if j == STEPS - 1:
                            link(ins)
                        if j % 4 == 3:
                            yield
                    for j in range(0, STEPS, 2):
                        nc.vector.reciprocal(w_[:, j * CHUNK:(j + 2) * CHUNK].rearrange("p (j t) -> p j t", t=CHUNK),
                                             prod[d][:, j:j + 2, 1:])
                        yield
                    nc.vector.tensor_copy(p_end[:, n % 2, d, :], prod[d][:, :, CHUNK]).then_inc(s.products_ready, 1)
                    dve.wait_ge(s.products_ready, 2 * n + d + 1)
                    if eng_is_vector(n, d):
                        dve.wait_ge(s.kk_normed, 1)
                        direction(n, d, dve, tt, ts, link, o_norm)
                if g == 3 and was >= 0:
                    dve.wait_ge(s.act_taken, SCAN.taken(("o_var", was)))
                    yield from inverse(o_norm, s.o_inverse)

            def take_side_tiles(q):
                pair, g = divmod(q, GROUPS)
                if (g == 0 and 0 < pair < PAIRS) or q == 1:
                    name = ("bonus", pair)
                    take2(SCAN, tt(rkv[:, pair, :], full2(SCAN, name), rkv[:, 2 * DC + pair, :], ALU.mult), name)
                if g == 2 and pair >= 1:
                    name = ("o_mean", pair - 1)
                    o_ = rkv[:, DC + pair - 1, :]
                    take2(SCAN, tt(o_, o_, full2(SCAN, name), ALU.subtract), name)

            for q in range(-GROUPS, 0):
                for _ in side(q):
                    pass

            bank0 = psum[:, 0, :].rearrange("p (i u t) -> p i u t", i=2, u=4)

            def mask(name):
                return c_view(name).unsqueeze(1).to_broadcast([P, 4, CONST[name].shape[1]])

            def take_z(k):
                dve.wait_ge(s.z_full, k + 1)
                q, jj = divmod(k, 2)
                if jj == 0:
                    dve.wait_ge(s.act_taken, SCAN.taken(("kv", q)))
                tt(z_buf[:, 0, :], psum[:, 5, 0:P], kv_buf[q % 2][:, jj * P:(jj + 1) * P], ALU.add).then_inc(s.z_taken, 1)

            def update_state(q, jj):
                pair, g = divmod(q, GROUPS)
                step = 2 * g + jj
                dve.wait_ge(s.os_full, 2 * q + jj + 1)
                if step == STEPS - 1:
                    nc.vector.memset(s_state, 0.0).then_inc(s.s_updated, 1)
                    return
                link(tt(s_state, psum[:, 2, 0:P].rearrange("p (u t) -> p u t", u=2), s_state, ALU.add))
                tt(s_state, s_state, p_end[:, pair % 2, :, step:step + 1].to_broadcast([P, 2, HEAD]),
                   ALU.mult).then_inc(s.s_updated, 1)

            for q in range(PAIRS * GROUPS + 1):
                small = side(q)
                pair, g = divmod(q, GROUPS)
                par = q % 2
                take_side_tiles(q)
                if q == PAIRS * GROUPS:
                    for jj in range(2):
                        take_z(2 * (q - 1) + jj)
                        update_state(q - 1, jj)
                    for _ in small:
                        pass
                    break
                dve.wait_ge(s.gram_full, q + 1)
                y_ = yi[:, par, :, :]
                for i, dst, name in ((0, xi, "minus_below0"), (1, y_, "minus_above0"), (1, ltm, "earlier")):
                    for h, rows in enumerate((slice(0, HEAD), slice(HEAD, P))):
                        ins = tt(dst[rows, :, h * HEAD:(h + 1) * HEAD], bank0[rows, i, :, :], mask(name)[rows, :, :],
                                 ALU.mult)
                link(ins)
                tt(xi, xi, mask("identity"), ALU.add)
                tt(y_, y_, mask("identity"), ALU.add).then_inc(s.xy_updated, 1)
                dve.wait_ge(s.stack_full, q + 1)
                for jj in range(2):
                    ins = tt(gram[:, par, 2 * jj:2 * jj + 2, :, :].rearrange("p u h t -> p (u h) t"),
                             psum[:, 1 + jj, :].rearrange("p (u t) -> p u t", u=4), mask("writes_before"), ALU.mult)
                ins.then_inc(s.gram_taken, 1)
                if q >= 1:
                    take_z(2 * (q - 1))
                for level in range(1, LEVELS):
                    for jj in range(2):
                        dve.wait_ge(s.t1_full, masked_step(q, level, jj))
                        tt(half(t1, jj), half(ps_t1[jj], 0), mask(f"below{level}"), ALU.mult).then_inc(s.t1_masked, 1)
                    if q >= 1 and level == 4:
                        update_state(q - 1, 1)
                    next(small, None)
                    for jj in range(2):
                        dve.wait_ge(s.xy_full, masked_step(q, level, jj))
                        y_part, x_part = y_[:, 2 * jj:2 * jj + 2, :], xi[:, 2 * jj:2 * jj + 2, :]
                        ins = tt(y_part, y_part, ps_y[jj], ALU.subtract)
                        if level < LEVELS - 1:
                            ins = tt(x_part, x_part, ps_x[jj], ALU.subtract)
                        ins.then_inc(s.xy_updated, 1)
                    if q >= 1 and level == 1:
                        update_state(q - 1, 0)
                    if q >= 1 and level == 2:
                        take_z(2 * (q - 1) + 1)
                    next(small, None)
                for _ in small:
                    pass
            for q in range(PAIRS * GROUPS + 1, (PAIRS + 1) * GROUPS):
                take_side_tiles(q)
                for _ in side(q):
                    pass

            def tile_b(*name, n=T2):
                return full2(SECOND_B, name, n)

            def take_b(ins, *name, wait=True):
                take2(SECOND_B, ins, name, wait)

            link(ts(subln, p2_col("subln", 0), 1.0 - LAM_INIT, None, ALU.mult))
            tt(lam_cols[0:HEAD, 0:2], lam_vec[0:HEAD, 0::2], lam_vec[0:HEAD, 1::2], ALU.mult).then_inc(s.lam_in, 1)
            for m in range(DC):
                src = tile_b("rw_out", m)
                for c in range(2):
                    part = slice(c * T, (c + 1) * T)
                    ins = stt(xx[:, m, part], src[:, part], mod[:, 0, 2 * DC + m, c:c + 1], xx[:, m, part],
                              ALU.mult, ALU.add)
                take_b(ins, "rw_out", m, wait=False)
            dve.wait_ge(s.dve_taken, SECOND_B.taken(("rw_out", DC - 1)))
            modulated_norm(1, SECOND_B, ("da", "mean_square"))
            rope_cos, rope_sin = c_view("rope_cos"), c_view("rope_sin")
            for no, (kind, x_all, n) in enumerate((("k", k_all, T2), ("q", q_all, T))):
                for h in range(DA_HEADS + 1):
                    if h < DA_HEADS:
                        dve.wait_ge(s.act_taken, SECOND_B.taken((kind + "_mean_square", h)))
                        norm = norms[:, h % 2, 0:n]
                        link(nc.vector.reciprocal(norm, norm))
                        stt(x_all[:, h, :], x_all[:, h, :], p2_col(kind + "n", 0), norm, ALU.mult,
                            ALU.mult).then_inc(s.scaled, 1)
                    if h >= 1:
                        x_ = x_all[:, h - 1, n - T:]
                        src = tile_b(kind + "_turned", h - 1, n=T)
                        take_b(tt(turned_sin, src, rope_sin, ALU.mult), kind + "_turned", h - 1)
                        link(tt(x_, x_, rope_cos, ALU.mult))
                        if kind == "k":
                            tt(x_, x_, turned_sin, ALU.add).then_inc(s.turned_in, 1)
                        else:
                            if h == 1:
                                dve.wait_ge(s.q_zeroed, 1)
                            for c, rows in enumerate((slice(0, HEAD), slice(HEAD, P))):
                                ins = tt(q_of[rows, c, h - 1, :], x_[rows, :], turned_sin[rows, :], ALU.add)
                            ins.then_inc(s.turned_in, 1)
                        dve.wait_ge(s.turned_in, no * DA_HEADS + h)
            dve.wait_ge(s.act_taken, SECOND_B.taken(("lam",)))
            link(tt(lam_cols[:, 4:5], lam_cols[:, 3:4], lam_cols[:, 2:3], ALU.subtract))
            link(ts(lam_cols[:, 5:6], lam_cols[:, 4:5], LAM_INIT, None, ALU.subtract))

            def take_output(h):
                take_b(nc.vector.tensor_copy(attn[:, h, :], tile_b("o", h, n=T)), "o", h)

            for i in range(2 * DA_HEADS + 1):
                if i < 2 * DA_HEADS:
                    for c in range(2):
                        link(nc.vector.tensor_reduce(maxima[:, i % 2, c:c + 1], tile_b("scores", i, c), AX_X, ALU.max))
                    ts(maxima[:, i % 2, :], maxima[:, i % 2, :], -SCALE, None, ALU.mult).then_inc(s.max_ready, 1)
                if i >= 1:
                    was, b = i - 1, (i - 1) % 2
                    dve.wait_ge(s.act_taken, SECOND_B.taken(("scores", was, 1)))
                    link(nc.vector.reciprocal(sums[:, b, :], sums[:, b, :]))
                    link(tt(sums[:, b, 1:2], sums[:, b, 1:2], lam_cols[:, 5:6], ALU.mult))
                    link(ts(probs[:, b, 0, :], probs[:, b, 0, :], sums[:, b, 0:1], None, ALU.mult))
                    stt(probs[:, b, 0, :], probs[:, b, 1, :], sums[:, b, 1:2], probs[:, b, 0, :], ALU.mult,
                        ALU.add).then_inc(s.probs_ready, 1)
                    if i >= 3 and i % 2 == 1:
                        take_output(i // 2 - 1)
                    h, qb = divmod(was, 2)
                    take_b(nc.vector.tensor_copy(probs_t[:, h % 2, :, qb * P:(qb + 1) * P],
                                                 tile_b("probs_turned", was).rearrange("p (c q) -> p c q", c=4)),
                           "probs_turned", was, wait=False)
            take_output(DA_HEADS - 1)
            for h in range(DA_HEADS):
                dve.wait_ge(s.act_taken, SECOND_B.taken(("o_mean_square", h)))
                link(nc.vector.reciprocal(norms[:, h % 2, 0:T], norms[:, h % 2, 0:T]))
                link(stt(attn[:, h, :], attn[:, h, :], subln, norms[:, h % 2, 0:T], ALU.mult, ALU.mult))
                tt(attn[:, h, :], attn[:, h, :], g_all[:, h, :], ALU.mult).then_inc(s.attn_ready, 1)
            for m in range(DC):
                src = tile_b("da_out", m, n=T)
                take_b(stt(xx[:, m, T:], src, mod[:, 1, 2 * DC + m, 1:2], xx[:, m, T:], ALU.mult, ALU.add),
                       "da_out", m, wait=False)


def tiles(w):
    k, m = w.shape
    return w.reshape(k // P, P, m // P, P).transpose(2, 0, 1, 3)


def by_column(a):
    return np.ascontiguousarray(a).reshape(-1, P).T


def kernel(**inputs):
    import concourse.bacc as bacc
    from concourse.bass_utils import run_bass_kernel_spmd

    a = {k: np.asarray(v_) for k, v_ in inputs.items()}
    parts = []
    for l in range(LAYERS):
        part = []

        def feed_forward(ffn):
            up = tiles(a[ffn + "_w_up"][l])
            for j in range(FC):
                part.append(up[j])
                part.append(up[FC + j])
            part.extend(tiles(a[ffn + "_w_down"][l]))

        feed_forward("ffn1")
        w_in = tiles(a["w_in"][l])
        lru0, gelu0, g0 = PG, PG + LH, PG + 2 * LH
        part.extend(w_in[lru0:lru0 + LH])
        part.extend(w_in[:PG])
        part.extend(w_in[gelu0:gelu0 + LH])
        for h in range(LH):
            part.append(a["lru_w_a"][l, h][None])
            part.append(a["lru_w_x"][l, h][None])
        for m in range(2 * DC):
            part.append(w_in[g0 + m])
            if m < PG:
                part.append(a["pool_w"][l, m][None])
        part.extend(tiles(a["w_pool_up"][l]))
        part.extend(tiles(a["w_lru_up"][l]))
        part.extend(tiles(a["w_out"][l]))
        feed_forward("ffn2")
        part = np.concatenate(part)
        assert len(part) == FIRST_TILES
        pad = np.zeros((FIRST_SLOTS * SLOT_TILES - len(part), P, P), np.float32)
        parts += [part, pad]
    rw_in = tiles(a["rw_in_2"][0])
    second = [rw_in[4 * DC:], rw_in[:3 * DC], rw_in[3 * DC:4 * DC]]
    second = np.concatenate([t_.reshape(-1, P, P) for t_ in second])
    assert len(second) == SECOND_A_TILES
    parts += [second, np.zeros((SECOND_A_SLOTS * SLOT_TILES - len(second), P, P), np.float32)]
    da_in = tiles(a["da_in_2"][0])
    third = np.concatenate([t_.reshape(-1, P, P) for t_ in (
        tiles(a["rw_out_2"][0]), da_in[DC:2 * DC], da_in[:DC], da_in[2 * DC:], tiles(a["da_out_2"][0]))])
    assert len(third) == SECOND_B_TILES
    parts += [third, np.zeros((SECOND_B_SLOTS * SLOT_TILES - len(third), P, P), np.float32)]
    stream = np.concatenate(parts)
    stream = np.ascontiguousarray(stream.reshape(-1, SLOT_TILES, P, P).transpose(0, 2, 1, 3)).reshape(
        -1, P, SLOT_TILES * P)

    ada = np.ascontiguousarray(np.concatenate([tiles(w) for w in a["ada_w_2"]]).transpose(0, 2, 1, 3))

    def feature_major(v_):
        return np.ascontiguousarray(v_.reshape(T, DC, P).transpose(2, 1, 0))

    p1 = np.concatenate([np.concatenate([by_column(a[n][l]) for n in (
        "norm_ffn1", "norm_mix", "norm_ffn2", "pool_b", "pool_scale", "conv_w", "conv_b", "lru_b_a", "lru_b_x")], 1)
        for l in range(LAYERS)], 1)
    lam = np.concatenate([by_column(a["lru_lambda"]), by_column(a["final_norm"])], 1)
    p2 = np.concatenate([by_column(a[n + "_2"]) for n in (
        "norm_g", "ada_b", "rw_mu", "rw_w0", "rw_a0", "rw_kk", "rw_ka", "rw_rk", "rw_gn_g", "rw_gn_b")]
        + [np.tile(a["da_qn_2"][0], 2)[:, None], np.tile(a["da_kn_2"][0], 2)[:, None], a["da_subln_2"].T], 1)
    assert p2.shape[1] == NP2
    c_vecs = np.stack([by_column(a["c_ctx_2"]), by_column(a["c_2"])], 2)
    lora = np.stack([a["rw_w2_2"][0].reshape(P, PAIRS, P), a["rw_a2_2"][0].reshape(P, PAIRS, P)], 1)
    arrays = {
        "weights": stream, "ada": ada, "x": feature_major(a["x"]), "p1": np.ascontiguousarray(p1),
        "lam": np.ascontiguousarray(lam), "const": np.ascontiguousarray(np.concatenate(list(CONST.values()), 1)),
        "ctx": feature_major(a["ctx_2"]), "p2": np.ascontiguousarray(p2), "c": np.ascontiguousarray(c_vecs),
        "lora": np.ascontiguousarray(lora), "lam_vec": np.ascontiguousarray(a["da_lam_2"][0].T),
    }
    nc = bacc.Bacc("TRN2", target_bir_lowering=False, num_devices=1)
    args = [nc.dram_tensor("in_" + n, v_.shape, F32, kind="ExternalInput").ap() for n, v_ in arrays.items()]
    out = nc.dram_tensor("out", (P, DC, T), F32, kind="ExternalOutput").ap()
    build(nc, *args, out)
    r = run_bass_kernel_spmd(nc, [{"in_" + n: v_ for n, v_ in arrays.items()}], core_ids=[0])
    got = r.results[0]["out"]
    return got.transpose(2, 1, 0).reshape(1, T, D)
```
